# Optimizing a Trainium2 kernel written in Bass

```python
import math
import jax, jax.numpy as jnp
from jax import lax
import numpy as np

D_MODEL = 1024
BATCH = 1
SEQ = 256
DEPTH = 1

GRID_W = 64
HEAD_DIM = 64
NA_HEADS = 8
NA_KH_MAX = 8
NA_KW = 16
NA_WIDTH = NA_HEADS * HEAD_DIM
SWA_Q_HEADS = 8
SWA_KV_HEADS = 2
SWA_WINDOW = 128
SWA_BLOCK = 128
SWA_Q_WIDTH = SWA_Q_HEADS * HEAD_DIM
SWA_KV_WIDTH = SWA_KV_HEADS * HEAD_DIM
ROPE_THETA = 500000.0
ROPE_DIM = HEAD_DIM // 4
D_FF = 4 * D_MODEL
IN_WIDTH = 3 * NA_WIDTH + SWA_Q_WIDTH + 2 * SWA_KV_WIDTH + 2 * D_MODEL
IN_SPLITS = [
    NA_WIDTH,
    2 * NA_WIDTH,
    3 * NA_WIDTH,
    3 * NA_WIDTH + SWA_Q_WIDTH,
    3 * NA_WIDTH + SWA_Q_WIDTH + SWA_KV_WIDTH,
    3 * NA_WIDTH + SWA_Q_WIDTH + 2 * SWA_KV_WIDTH,
    3 * NA_WIDTH + SWA_Q_WIDTH + 2 * SWA_KV_WIDTH + D_MODEL,
]
DEEPNORM_ALPHA = (2.0 * DEPTH) ** 0.25
DEEPNORM_BETA = (8.0 * DEPTH) ** -0.25
LN_EPS = 1e-5
MASK_VALUE = -1e30


def layer_norm(x, g, b):
    xf = x.astype(jnp.float32)
    mu = jnp.mean(xf, axis=-1, keepdims=True)
    xc = xf - mu
    var = jnp.mean(xc * xc, axis=-1, keepdims=True)
    y = xc * lax.rsqrt(var + LN_EPS) * g.astype(jnp.float32) + b.astype(jnp.float32)
    return y.astype(x.dtype)

def partial_rotary(x, pos):
    half = ROPE_DIM // 2
    inv_freq = jnp.power(ROPE_THETA, -jnp.arange(0, ROPE_DIM, 2, dtype=jnp.float32) / ROPE_DIM)
    ang = pos.astype(jnp.float32)[:, None] * inv_freq[None, :]
    cos = jnp.cos(ang)[:, None, :]
    sin = jnp.sin(ang)[:, None, :]
    xr = x[..., :ROPE_DIM].astype(jnp.float32)
    x1, x2 = xr[..., :half], xr[..., half:]
    rot = jnp.concatenate([x1 * cos - x2 * sin, x2 * cos + x1 * sin], axis=-1)
    return jnp.concatenate([rot.astype(x.dtype), x[..., ROPE_DIM:]], axis=-1)

def neighbourhood_attention(q, k, v, rpb):
    B, S, H, Dh = q.shape
    rows = S // GRID_W
    kh = min(NA_KH_MAX, rows)
    kw = NA_KW
    qg = q.reshape(B, rows, GRID_W, H, Dh)
    kg = k.reshape(B, rows, GRID_W, H, Dh)
    vg = v.reshape(B, rows, GRID_W, H, Dh)
    cols = jnp.arange(GRID_W)
    col_start = jnp.clip(cols - kw // 2, 0, GRID_W - kw)
    col_idx = col_start[:, None] + jnp.arange(kw)[None, :]
    dc = col_idx - cols[:, None]
    scale = Dh ** -0.5

    def one_row(r):
        rs = jnp.clip(r - kh // 2, 0, rows - kh)
        kr = lax.dynamic_slice_in_dim(kg, rs, kh, axis=1)
        vr = lax.dynamic_slice_in_dim(vg, rs, kh, axis=1)
        kn = kr[:, :, col_idx]
        vn = vr[:, :, col_idx]
        qr = lax.dynamic_index_in_dim(qg, r, axis=1, keepdims=False)
        s = jnp.einsum('bwhd,bkwjhd->bhwkj', qr, kn).astype(jnp.float32) * scale
        dr = rs + jnp.arange(kh) - r
        bias = rpb[:, (dr + NA_KH_MAX - 1)[None, :, None], (dc + kw - 1)[:, None, :]]
        s = s + bias.astype(jnp.float32)[None]
        p = jax.nn.softmax(s.reshape(B, H, GRID_W, kh * kw), axis=-1)
        p = p.reshape(B, H, GRID_W, kh, kw).astype(v.dtype)
        return jnp.einsum('bhwkj,bkwjhd->bwhd', p, vn)

    out = lax.map(one_row, jnp.arange(rows))
    return jnp.moveaxis(out, 0, 1).reshape(B, S, H * Dh)

def windowed_gqa_with_sink(q, k, v, sink):
    B, S, Hq, Dh = q.shape
    G = k.shape[2]
    rep = Hq // G
    blk = SWA_BLOCK
    nb = S // blk
    qb = q.reshape(B, nb, blk, G, rep, Dh)
    pad = ((0, 0), (blk, blk), (0, 0), (0, 0))
    kp = jnp.pad(k, pad).reshape(B, nb + 2, blk, G, Dh)
    vp = jnp.pad(v, pad).reshape(B, nb + 2, blk, G, Dh)
    kb = jnp.concatenate([kp[:, :-2], kp[:, 1:-1], kp[:, 2:]], axis=2)
    vb = jnp.concatenate([vp[:, :-2], vp[:, 1:-1], vp[:, 2:]], axis=2)
    s = jnp.einsum('bnqgrd,bnkgd->bngrqk', qb, kb).astype(jnp.float32) * (Dh ** -0.5)
    qpos = jnp.arange(nb)[:, None] * blk + jnp.arange(blk)[None, :]
    kpos = jnp.arange(nb)[:, None] * blk - blk + jnp.arange(3 * blk)[None, :]
    rel = kpos[:, None, :] - qpos[:, :, None]
    valid = (jnp.abs(rel) <= SWA_WINDOW) & (kpos[:, None, :] >= 0) & (kpos[:, None, :] < S)
    s = jnp.where(valid[None, :, None, None], s, MASK_VALUE)
    sink_l = sink.astype(jnp.float32).reshape(1, 1, G, rep, 1, 1)
    m = jnp.maximum(jnp.max(s, axis=-1, keepdims=True), sink_l)
    e = jnp.exp(s - m)
    p = e / (jnp.sum(e, axis=-1, keepdims=True) + jnp.exp(sink_l - m))
    o = jnp.einsum('bngrqk,bnkgd->bnqgrd', p.astype(v.dtype), vb)
    return o.reshape(B, S, Hq * Dh)

def first_inputs(seed: int = 0) -> dict:
    key = jax.random.key(seed)
    ks = jax.random.split(key, 24)
    f32 = jnp.float32
    beta = DEEPNORM_BETA

    def nrm(k, shape, scale):
        return jax.random.normal(k, shape, f32) * scale

    col_scale = jnp.concatenate([
        jnp.ones((2 * NA_WIDTH,), f32), jnp.full((NA_WIDTH,), beta, f32),
        jnp.ones((SWA_Q_WIDTH + SWA_KV_WIDTH,), f32), jnp.full((SWA_KV_WIDTH,), beta, f32),
        jnp.ones((2 * D_MODEL,), f32)])
    w_in = nrm(ks[1], (DEPTH, D_MODEL, IN_WIDTH), D_MODEL ** -0.5) * col_scale
    return {
        "x": jax.random.normal(ks[0], (BATCH, SEQ, D_MODEL), f32),
        "ln0_g": 1.0 + nrm(ks[2], (D_MODEL,), 0.05),
        "ln0_b": nrm(ks[3], (D_MODEL,), 0.02),
        "w_in": w_in,
        "b_in": nrm(ks[4], (DEPTH, IN_WIDTH), 0.02),
        "na_rpb": nrm(ks[5], (DEPTH, NA_HEADS, 2 * NA_KH_MAX - 1, 2 * NA_KW - 1), 0.1),
        "swa_sink": nrm(ks[6], (DEPTH, SWA_Q_HEADS), 0.5),
        "w_branch_na": nrm(ks[7], (DEPTH, NA_WIDTH, D_MODEL), NA_WIDTH ** -0.5 * beta),
        "w_branch_swa": nrm(ks[8], (DEPTH, SWA_Q_WIDTH, D_MODEL), SWA_Q_WIDTH ** -0.5 * beta),
        "w_out": nrm(ks[9], (DEPTH, D_MODEL, D_MODEL), D_MODEL ** -0.5 * beta),
        "b_out": nrm(ks[10], (DEPTH, D_MODEL), 0.02),
        "ln1_g": 1.0 + nrm(ks[11], (DEPTH, D_MODEL), 0.05),
        "ln1_b": nrm(ks[12], (DEPTH, D_MODEL), 0.02),
        "w_ff1": nrm(ks[13], (DEPTH, D_MODEL, D_FF), D_MODEL ** -0.5 * beta),
        "b_ff1": nrm(ks[14], (DEPTH, D_FF), 0.02),
        "w_ff2": nrm(ks[15], (DEPTH, D_FF, D_MODEL), D_FF ** -0.5 * beta),
        "b_ff2": nrm(ks[16], (DEPTH, D_MODEL), 0.02),
        "ln2_g": 1.0 + nrm(ks[17], (DEPTH, D_MODEL), 0.05),
        "ln2_b": nrm(ks[18], (DEPTH, D_MODEL), 0.02),
    }

def first_block(x, ln0_g, ln0_b, w_in, b_in, na_rpb, swa_sink, w_branch_na, w_branch_swa,
              w_out, b_out, ln1_g, ln1_b, w_ff1, b_ff1, w_ff2, b_ff2, ln2_g, ln2_b):
    B, S, _ = x.shape
    pos = jnp.arange(S)
    h = layer_norm(x, ln0_g, ln0_b)
    for l in range(DEPTH):
        proj = h @ w_in[l] + b_in[l]
        qa, ka, va, qb, kb, vb, ga, gb = jnp.split(proj, IN_SPLITS, axis=-1)
        qa = qa.reshape(B, S, NA_HEADS, HEAD_DIM)
        ka = ka.reshape(B, S, NA_HEADS, HEAD_DIM)
        va = va.reshape(B, S, NA_HEADS, HEAD_DIM)
        qb = partial_rotary(qb.reshape(B, S, SWA_Q_HEADS, HEAD_DIM), pos)
        kb = partial_rotary(kb.reshape(B, S, SWA_KV_HEADS, HEAD_DIM), pos)
        vb = vb.reshape(B, S, SWA_KV_HEADS, HEAD_DIM)
        y_na = neighbourhood_attention(qa, ka, va, na_rpb[l]) @ w_branch_na[l]
        y_swa = windowed_gqa_with_sink(qb, kb, vb, swa_sink[l]) @ w_branch_swa[l]
        mixed = jax.nn.sigmoid(ga) * y_na + jax.nn.sigmoid(gb) * y_swa
        attn_out = mixed @ w_out[l] + b_out[l]
        h = layer_norm(DEEPNORM_ALPHA * h + attn_out, ln1_g[l], ln1_b[l])
        u = jnp.square(jax.nn.relu(h @ w_ff1[l] + b_ff1[l]))
        ffn_out = u @ w_ff2[l] + b_ff2[l]
        h = layer_norm(DEEPNORM_ALPHA * h + ffn_out, ln2_g[l], ln2_b[l])
    return h


DEPTH_2 = 2

N_A = DEPTH_2 // 2
N_B = DEPTH_2 - N_A
POOL_WINDOWS = (2, 4, 8, 16)
N_POOL_GROUPS = len(POOL_WINDOWS)
GROUP_CH = D_MODEL // N_POOL_GROUPS
N_Q_HEADS = D_MODEL // HEAD_DIM
N_KV_HEADS = 4
Q_PER_KV = N_Q_HEADS // N_KV_HEADS
WINDOW = 128
BLOCK = 128
ROPE_THETA_2 = 10000.0
ATTN_SCALE = 1.0 / math.sqrt(HEAD_DIM)
NEG_INF = -1e30
D_FF_2 = 2816
CONV_WIDTH = 3
RMS_EPS = 1e-6


def rms_norm(x, g):
    xf = x.astype(jnp.float32)
    y = xf * lax.rsqrt(jnp.mean(xf * xf, axis=-1, keepdims=True) + RMS_EPS)
    return (y * g.astype(jnp.float32)).astype(x.dtype)

def pool_mixer(h, w_pool, scale):
    B, S, D = h.shape
    hf = h.astype(jnp.float32)
    csum = jnp.concatenate([jnp.zeros((B, 1, D), jnp.float32), jnp.cumsum(hf, axis=1)], axis=1)
    t = jnp.arange(1, S + 1)
    diffs = []
    for gi, w in enumerate(POOL_WINDOWS):
        sl = slice(gi * GROUP_CH, (gi + 1) * GROUP_CH)
        lo = jnp.maximum(t - w, 0)
        cnt = jnp.minimum(t, w).astype(jnp.float32)
        mean = (csum[:, 1:, sl] - csum[:, lo, sl]) / cnt[None, :, None]
        diffs.append(mean - hf[..., sl])
    d = jnp.stack(diffs, axis=2).astype(h.dtype)
    y = jnp.einsum('bsgc,gcd->bsgd', d, w_pool).reshape(B, S, D)
    return y * scale

def conv_glu_ffn(h, w_in, conv_w, conv_b, w_out):
    S = h.shape[1]
    u = h @ w_in
    up = jnp.pad(u, ((0, 0), (CONV_WIDTH - 1, 0), (0, 0)))
    u = sum(conv_w[k] * up[:, k:k + S] for k in range(CONV_WIDTH)) + conv_b
    gate, val = jnp.split(u, 2, axis=-1)
    return (jax.nn.gelu(gate, approximate=True) * val) @ w_out

def rope(x, cos, sin):
    xf = x.astype(jnp.float32)
    x1, x2 = jnp.split(xf, 2, axis=-1)
    return jnp.concatenate([x1 * cos - x2 * sin, x2 * cos + x1 * sin], axis=-1).astype(x.dtype)

def rope_tables(positions):
    inv_freq = 1.0 / (ROPE_THETA_2 ** (jnp.arange(0, HEAD_DIM, 2, dtype=jnp.float32) / HEAD_DIM))
    ang = positions.astype(jnp.float32)[..., None] * inv_freq
    return jnp.cos(ang)[:, :, None, :], jnp.sin(ang)[:, :, None, :]

def band_blocks(t):
    B, S = t.shape[:2]
    nb = S // BLOCK
    tb = t.reshape(B, nb, BLOCK, N_KV_HEADS, HEAD_DIM)
    prev = jnp.pad(tb, ((0, 0), (1, 0), (0, 0), (0, 0), (0, 0)))[:, :-1]
    return jnp.concatenate([prev, tb], axis=2).astype(jnp.float32)

def swa_sink_attention(q, kk, vv, sinks):
    B, S = q.shape[:2]
    nb = S // BLOCK
    qb = q.reshape(B, nb, BLOCK, N_KV_HEADS, Q_PER_KV, HEAD_DIM).astype(jnp.float32) * ATTN_SCALE
    s = jnp.einsum('bnqhgd,bnkhd->bnhgqk', qb, kk)
    qi = jnp.arange(BLOCK)[:, None]
    kj = jnp.arange(2 * BLOCK)[None, :]
    rel = BLOCK + qi - kj
    blk = jnp.arange(nb)[:, None, None]
    valid = (rel >= 0) & (rel < WINDOW) & (blk * BLOCK + kj - BLOCK >= 0)
    s = jnp.where(valid[None, :, None, None], s, NEG_INF)
    sink = sinks.astype(jnp.float32).reshape(N_KV_HEADS, Q_PER_KV)[None, None, :, :, None, None]
    m = jnp.maximum(jnp.max(s, axis=-1, keepdims=True), sink)
    p = jnp.exp(s - m)
    denom = jnp.sum(p, axis=-1) + jnp.exp(sink - m)[..., 0]
    o = jnp.einsum('bnhgqk,bnkhd->bnhgqd', p, vv) / denom[..., None]
    o = o.transpose(0, 1, 4, 2, 3, 5).reshape(B, S, N_Q_HEADS * HEAD_DIM)
    return o.astype(q.dtype)

def second_inputs(seed: int = 0) -> dict:
    key = jax.random.key(seed)
    ks = jax.random.split(key, 20)
    f32 = jnp.float32
    D, F = D_MODEL, D_FF_2
    HQD, HKVD = N_Q_HEADS * HEAD_DIM, N_KV_HEADS * HEAD_DIM

    def gain(k, shape):
        return 1.0 + 0.05 * jax.random.normal(k, shape, f32)

    x = jax.random.normal(ks[0], (BATCH, SEQ, D), f32)
    positions = jnp.broadcast_to(jnp.arange(SEQ, dtype=jnp.int32)[None, :], (BATCH, SEQ))
    return {
        "x": x,
        "positions": positions,
        "mix_pre_g": gain(ks[1], (DEPTH_2, D)),
        "mix_post_g": gain(ks[2], (DEPTH_2, D)),
        "pool_w": jax.random.normal(ks[3], (N_A, N_POOL_GROUPS, GROUP_CH, GROUP_CH), f32) * GROUP_CH ** -0.5,
        "pool_scale": 1.0 + 0.1 * jax.random.normal(ks[4], (N_A, D), f32),
        "kv_norm_g": gain(ks[5], (D,)),
        "w_kv": jax.random.normal(ks[6], (D, 2 * HKVD), f32) * D ** -0.5,
        "w_q": jax.random.normal(ks[7], (N_B, D, HQD), f32) * D ** -0.5,
        "w_o": jax.random.normal(ks[8], (N_B, HQD, D), f32) * HQD ** -0.5,
        "sinks": jax.random.normal(ks[9], (N_B, N_Q_HEADS), f32),
        "ffn_pre_g": gain(ks[10], (DEPTH_2, D)),
        "ffn_post_g": gain(ks[11], (DEPTH_2, D)),
        "ffn_w_in": jax.random.normal(ks[12], (DEPTH_2, D, 2 * F), f32) * D ** -0.5,
        "ffn_conv_w": jax.random.normal(ks[13], (DEPTH_2, CONV_WIDTH, 2 * F), f32) * CONV_WIDTH ** -0.5,
        "ffn_conv_b": 0.01 * jax.random.normal(ks[14], (DEPTH_2, 2 * F), f32),
        "ffn_w_out": jax.random.normal(ks[15], (DEPTH_2, F, D), f32) * F ** -0.5,
    }

def second_block(x, positions, mix_pre_g, mix_post_g, pool_w, pool_scale, kv_norm_g, w_kv,
              w_q, w_o, sinks, ffn_pre_g, ffn_post_g, ffn_w_in, ffn_conv_w, ffn_conv_b, ffn_w_out):
    B, S, D = x.shape
    cos, sin = rope_tables(positions)
    kk = vv = None
    for layer in range(DEPTH_2):
        h = rms_norm(x, mix_pre_g[layer])
        if layer < N_A:
            m = pool_mixer(h, pool_w[layer], pool_scale[layer])
        else:
            if layer == N_A:
                hkv = rms_norm(x, kv_norm_g)
                kv = (hkv @ w_kv).reshape(B, S, 2, N_KV_HEADS, HEAD_DIM)
                k_shared = rope(kv[:, :, 0], cos, sin)
                kk, vv = band_blocks(k_shared), band_blocks(kv[:, :, 1])
            j = layer - N_A
            q = rope((h @ w_q[j]).reshape(B, S, N_Q_HEADS, HEAD_DIM), cos, sin)
            m = swa_sink_attention(q, kk, vv, sinks[j]) @ w_o[j]
        x = x + rms_norm(m, mix_post_g[layer])
        f = conv_glu_ffn(rms_norm(x, ffn_pre_g[layer]), ffn_w_in[layer], ffn_conv_w[layer],
                         ffn_conv_b[layer], ffn_w_out[layer])
        x = x + rms_norm(f, ffn_post_g[layer])
    return x


def setup_inputs(seed=0):
    out = dict(first_inputs(seed))
    for name, value in second_inputs(seed + 1).items():
        if name != "x":
            out[name + "_2"] = value
    return out


def reference(
    x, ln0_g, ln0_b, w_in, b_in, na_rpb, swa_sink, w_branch_na, w_branch_swa, w_out, b_out,
    ln1_g, ln1_b, w_ff1, b_ff1, w_ff2, b_ff2, ln2_g, ln2_b, positions_2, mix_pre_g_2,
    mix_post_g_2, pool_w_2, pool_scale_2, kv_norm_g_2, w_kv_2, w_q_2, w_o_2, sinks_2,
    ffn_pre_g_2, ffn_post_g_2, ffn_w_in_2, ffn_conv_w_2, ffn_conv_b_2, ffn_w_out_2,
):
    x = first_block(
        x, ln0_g, ln0_b, w_in, b_in, na_rpb, swa_sink, w_branch_na, w_branch_swa, w_out, b_out,
        ln1_g, ln1_b, w_ff1, b_ff1, w_ff2, b_ff2, ln2_g, ln2_b,
    )
    return second_block(
        x, positions_2, mix_pre_g_2, mix_post_g_2, pool_w_2, pool_scale_2, kv_norm_g_2, w_kv_2,
        w_q_2, w_o_2, sinks_2, ffn_pre_g_2, ffn_post_g_2, ffn_w_in_2, ffn_conv_w_2,
        ffn_conv_b_2, ffn_w_out_2,
    )


_drawn_inputs = setup_inputs


def setup_inputs(seed=0):
    import zlib

    import numpy as np

    out = dict(_drawn_inputs(seed))
    spreads = {}
    factors = {'b_in': 6.442,
     'na_rpb': 8.0,
     'swa_sink': 8.0,
     'w_branch_swa': 2.695,
     'b_ff1': 3.956,
     'sinks_2': 3.289,
     'ffn_conv_b_2': 3.724}
    for name, (base, spread) in spreads.items():
        noise = np.random.default_rng([zlib.crc32(name.encode()), seed]).standard_normal(out[name].shape)
        drawn = base * np.exp(spread * noise) if base else spread * noise
        out[name] = __import__('jax').numpy.asarray(drawn.astype(out[name].dtype))
    for name, factor in factors.items():
        out[name] = (out[name] * factor).astype(out[name].dtype)
    return out
```

```python
from contextlib import ExitStack

import numpy as np

import concourse.bass as bass
from concourse import mybir

F32 = mybir.dt.float32
F32R = mybir.dt.float32r
I32 = mybir.dt.int32
ALU = mybir.AluOpType
ACT = mybir.ActivationFunctionType
AX_X = mybir.AxisListType.X

P = 128
T = 256
TT = T // P
D = 1024
DC = D // P
HD = 64
HEADS_NA = 8
HEADS_SWA = 8
HEADS_2 = 16
GRID_W = 64
GRID_ROWS = T // GRID_W
KW = 16
F1 = 4096
F2 = 2816
ALPHA = float(2.0 ** 0.25)
LN_EPS = 1e-5
RMS_EPS = 1e-6
MASKED = -1e30
SCALE = float(HD) ** -0.5
POOL_WINDOWS = (2, 4, 8, 16)
PAD = POOL_WINDOWS[-1]

UNIT = 2048
UC = UNIT // DC
RING = 3
U_QKV = 0
U_GATE = U_QKV + 9
U_BRANCH = U_GATE + 8
U_WOUT = U_BRANCH + 4
U_FF = U_WOUT + 4
PAIRS1 = F1 // (2 * P)
U_POOL = U_FF + 2 * PAIRS1
U_GLU0 = U_POOL + 1
PAIRS2 = F2 // (2 * P)
U_KV = U_GLU0 + 3 * PAIRS2
U_Q = U_KV + 2
U_WO = U_Q + 4
U_GLU1 = U_WO + 4
N_UNITS = U_GLU1 + 3 * PAIRS2


def output_tile_units():
    units = list(range(U_QKV, U_BRANCH)) + list(range(U_WOUT, U_FF))
    units += [U_FF] + [U_FF + 1 + 2 * j for j in range(PAIRS1 - 1)]
    for base in (U_GLU0, U_GLU1):
        units += [base, base + 1]
        units += [base + 2 + 3 * j + k for j in range(PAIRS2 - 1) for k in (0, 1)]
    units += list(range(U_KV, U_GLU1))
    return sorted(units)


UP_INDEX = {n: q for q, n in enumerate(output_tile_units())}

OUT_MOST = 3

LN1, LN2, MIXPRE0, MIXPOST0, FFNPRE0, FFNPOST0, MIXPRE1, MIXPOST1, FFNPRE1, FFNPOST1 = range(10)
S_LN0 = 10
X_LN0, X_O1, X_MIXED, X_LN1, X_POOL, X_FFN0, X_KV, X_Q, X_O2, X_FFN1 = range(10)

SWA_ORDER = [0, 4, 1, 5, 2, 6, 3, 7]
ORDER_2 = [0, 4, 1, 5, 2, 6, 3, 7, 8, 12, 9, 13, 10, 14, 11, 15]

PARAM_WIDTHS = [
    ("ln0_g", DC), ("ln0_b", DC), ("b_in", 34), ("b_out", DC), ("ln1_g", DC), ("ln1_b", DC),
    ("b_ff1", F1 // P), ("b_ff2", DC), ("ln2_g", DC), ("ln2_b", DC),
    ("mix_pre0", DC), ("mix_pre1", DC), ("mix_post0", DC), ("mix_post1", DC), ("pool_scale", DC),
    ("kv_g", DC), ("ffn_pre0", DC), ("ffn_pre1", DC), ("ffn_post0", DC), ("ffn_post1", DC),
    ("conv0", 16 * PAIRS2), ("conv1", 16 * PAIRS2), ("sink1", HEADS_SWA), ("sink2", HEADS_2),
]
CONST_WIDTHS = [
    ("na_mask", GRID_W), ("swa_mask", P + T), ("mask2", P + T), ("cos1", T), ("sin1", T),
    ("perm1", P), ("perm2", P), ("pool_fix", 4 * PAD), ("inv_freq2", 1), ("sign2", 1),
]


def offsets(widths):
    at, out = 0, {}
    for name, w in widths:
        out[name] = at
        at += w
    return out, at


PAR, N_PAR = offsets(PARAM_WIDTHS)
CON, N_CON = offsets(CONST_WIDTHS)

TWO_PI_PARTS = (6.25, 0.03125, 0.001934051513671875, 1.2556659146e-6)
ROUND_MAGIC = 12582912.0
PI_BELOW = 3.1415925


class Chain:

    def __init__(self, eng, sem):
        self.eng, self.sem, self.n, self.offset = eng, sem, 0, 0

    def link(self, ins):
        ins.then_inc(self.sem, 1)
        self.n += 1
        self.eng.wait_ge(self.sem, self.n + self.offset)

    def enter(self, i, steps):
        self.start, self.steps, self.offset = self.n, steps, i * steps

    def leave(self, rounds):
        assert self.n - self.start == self.steps, (self.n - self.start, self.steps)
        self.n, self.offset = self.start + rounds * self.steps, 0


class Straight:

    def unit(self, n):
        return n

    def landed(self, n):
        return 16 * (n // RING + 1)

    def up(self, q):
        return q

    def pair(self, j):
        return j


class Looped:

    def __init__(self, i, ups, pairs):
        self.i, self.ups, self.pairs = i, ups, pairs

    def unit(self, n):
        return n + 6 * self.i

    def landed(self, n):
        return 16 * (n // RING + 1) + 32 * self.i

    def up(self, q):
        return q + self.ups * self.i

    def pair(self, j):
        return j + self.pairs * self.i


STRAIGHT = Straight()
GLU_ROUNDS = (PAIRS2 - 5) // 2


def build(nc, x, w_stream, params, consts, rpb, positions, out):
    ctx = ExitStack()
    with ctx:
        def sb(name, shape, dt=F32):
            return ctx.enter_context(nc.sbuf_tensor(name, shape, dt))

        def sem(name):
            return ctx.enter_context(nc.semaphore(name))

        w32 = [sb(f"w32_{s}", [P, UNIT]) for s in range(RING)]
        w_hi = [sb(f"w_hi{s}", [P, UNIT], F32R) for s in range(RING)]
        w_lo = [sb(f"w_lo{s}", [P, UNIT], F32R) for s in range(RING)]
        x_hi = [sb(f"x_hi{s}", [P, DC, T], F32R) for s in range(2)]
        x_lo = [sb(f"x_lo{s}", [P, DC, T], F32R) for s in range(2)]
        mid_hi = [sb(f"mid_hi{s}", [P, 2, T], F32R) for s in range(3)]
        mid_lo = [sb(f"mid_lo{s}", [P, 2, T], F32R) for s in range(3)]
        par = sb("par", [P, N_PAR])
        con = sb("con", [P, N_CON])
        ident = sb("ident", [P, P])
        inv_d = sb("inv_d", [P, 1])
        neg_half = sb("neg_half", [P, TT])
        half_gate_bias = sb("half_gate_bias", [P, 2 * DC])
        neg_sink1 = sb("neg_sink1", [P, HEADS_SWA])
        neg_sink2 = sb("neg_sink2", [P, HEADS_2])
        cos2 = sb("cos2", [P, T])
        sin2 = sb("sin2", [P, T])
        res = sb("res", [P, DC, T])
        proj = sb("proj", [P, 18, T])
        raw = proj[:, 0:DC, :]
        sq = proj[:, DC:2 * DC, :]
        rows = [sb(f"rows{s}", [P, 2 * T]) for s in range(2)]
        stat = sb("stat", [P, 11, 8])
        v_tok = sb("v_tok", [P, TT, HEADS_NA * HD])
        v_tok_swa = sb("v_tok_swa", [P, TT, P])
        BIAS_ROWS = GRID_ROWS + 2
        BIAS_W = BIAS_ROWS * GRID_W
        REGION = max(HEADS_NA * BIAS_W, 3104)
        region = sb("region", [P, REGION])
        bias_na = region[:, 0:HEADS_NA * BIAS_W].rearrange("p (h k) -> p h k", h=HEADS_NA)
        gates = sb("gates", [P, 2 * DC, T])
        scores = [sb(f"scores{s}", [P, 2 * T]) for s in range(2)]
        probs = [sb(f"probs{s}", [P, 2 * T]) for s in range(2)]
        probs_t = [sb(f"probs_t{s}", [P, 2 * T]) for s in range(2)]
        small = sb("small", [P, 5, 2 * 32])
        glu_u = [region[:, k * 2 * (T + 2):(k + 1) * 2 * (T + 2)].rearrange("p (t n) -> p t n", t=2)
                 for k in range(2)]
        glu_c = [region[:, 1056 + k * 2 * T:1056 + (k + 1) * 2 * T].rearrange("p (t n) -> p t n", t=2)
                 for k in range(2)]
        glu_g = region[:, 2080:2080 + 2 * T].rearrange("p (t n) -> p t n", t=2)
        glu_m = region[:, 2592:2592 + 2 * T].rearrange("p (t n) -> p t n", t=2)
        relu_v = glu_m
        gflat = gates[:, :, :].rearrange("p c n -> p (c n)")
        pooled = gflat[:, 0:DC * (T + PAD)].rearrange("p (c n) -> p c n", c=DC)
        run_a = gflat[:, DC * (T + PAD):DC * (T + PAD) + 2 * (T + PAD)].rearrange("p (c n) -> p c n", c=2)
        run_b = gflat[:, DC * (T + PAD) + 2 * (T + PAD):DC * (T + PAD) + 4 * (T + PAD)].rearrange("p (c n) -> p c n", c=2)
        x_tok = gates[:, 0:8, :].rearrange("p (t c) n -> p t (c n)", t=TT)
        xn_tok = gates[:, 8:16, :].rearrange("p (t c) n -> p t (c n)", t=TT)
        out_tok = x_tok
        pos_i = probs[0][:, 0:T].bitcast(I32)
        tmp_rot = [gates[:, 12:14, :], gates[:, 14:16, :]]
        angle = [scores[0][:, 0:T], scores[0][:, T:2 * T], scores[1][:, 0:T], scores[1][:, T:2 * T]]
        v_tok2 = v_tok[:, :, 0:4 * HD]

        up = [ctx.enter_context(nc.psum_tensor(f"up{b}", [P, 2 * T], F32)) for b in range(RING)]
        aux = ctx.enter_context(nc.psum_tensor("aux", [P, 2 * T], F32))
        down = [ctx.enter_context(nc.psum_tensor(f"down{b}", [P, 2 * T], F32)) for b in range(4)]

        x_landed = sem("x_landed")
        par_landed = sem("par_landed")
        con_landed = sem("con_landed")
        pos_landed = sem("pos_landed")
        bias_landed = sem("bias_landed")
        w_landed = [sem(f"w_landed{s}") for s in range(RING)]
        w_hi_ready = sem("w_hi_ready")
        w_lo_ready = sem("w_lo_ready")
        unit_done = sem("unit_done")
        up_read = sem("up_read")
        x_hi_ready = sem("x_hi_ready")
        x_ready = sem("x_ready")
        const_ready = sem("const_ready")
        ident_zero = sem("ident_zero")
        small_ready = sem("small_ready")
        ln0_var = sem("ln0_var")
        ln0_rstd = sem("ln0_rstd")
        ln0_shift = sem("ln0_shift")
        xn_ready = sem("xn_ready")
        ln0_turned = sem("ln0_turned")
        ln0_h = sem("ln0_h")
        angle_ready = sem("angle_ready")
        trig_ready = sem("trig_ready")
        bias_ready = sem("bias_ready")
        dve_chain = sem("dve_chain")
        act_chain = sem("act_chain")
        pool_chain = sem("pool_chain")
        raw_ready = sem("raw_ready")
        sq_ready = sem("sq_ready")
        sum_ready = sem("sum_ready")
        mean_ready = sem("mean_ready")
        stat_done = sem("stat_done")
        var_ready = sem("var_ready")
        rstd_ready = sem("rstd_ready")
        shift_ready = sem("shift_ready")
        rows_done = sem("rows_done")
        rows_ready = sem("rows_ready")
        scaled_ready = sem("scaled_ready")
        pool_added = sem("pool_added")
        dve_added = sem("dve_added")
        res_ready = sem("res_ready")
        res_b_ready = sem("res_b_ready")
        rot_done = sem("rot_done")
        rot_read = sem("rot_read")
        rot_ready = sem("rot_ready")
        v_turned = sem("v_turned")
        v_ready = sem("v_ready")
        s_done = sem("s_done")
        s_ready = sem("s_ready")
        negmax_ready = sem("negmax_ready")
        p_ready = sem("p_ready")
        rden_ready = sem("rden_ready")
        pn_ready = sem("pn_ready")
        pt_done = sem("pt_done")
        pt_ready = sem("pt_ready")
        o_done = sem("o_done")
        mixed_ready = sem("mixed_ready")
        down_done = sem("down_done")
        relu_ready = sem("relu_ready")
        glu_ready = sem("glu_ready")
        conv_first = sem("conv_first")
        conv_ready = sem("conv_ready")
        gelu_ready = sem("gelu_ready")
        mid_f32 = sem("mid_f32")
        mid_hi_ready = sem("mid_hi_ready")
        mid_ready = sem("mid_ready")
        diff_ready = sem("diff_ready")
        out_turned = sem("out_turned")
        out_act_ready = sem("out_act_ready")
        out_dve_ready = sem("out_dve_ready")
        out_stored = sem("out_stored")

        block = ctx.enter_context(nc.Block())

        def pcol(name, c, n=1):
            return par[:, PAR[name] + c:PAR[name] + c + n]

        def pdyn(name, c, n=1):
            return par[:, bass.ds(PAR[name] + c, n)]

        def ccol(name, c=0, n=1):
            return con[:, CON[name] + c:CON[name] + c + n]

        def shifted(handle, width, offset):
            return bass.AP(handle[:, :].tensor, offset + P, [[width, P], [-P, 2], [1, T]])

        def pair_view(ap):
            return ap.rearrange("p (t n) -> p t n", t=2)

        def twice(ap):
            return ap.unsqueeze(1).to_broadcast([P, 2, T])

        def wait_added(e, index, gr):
            if index < 2:
                e.wait_ge((pool_added, dve_added)[gr // 2], 2 * index + gr % 2 + 1)
            elif gr == 0:
                e.wait_ge(dve_added, 4 + index - 2 + 1)
            else:
                e.wait_ge(pool_added, 4 + 3 * (index - 2) + gr)

        def add_group(engine, e, chain, total, values, step, wait_group):
            if step == 1:
                wait_group(0)
            wait_group(step)
            first = values[:, 0:2, :] if step == 1 else total
            chain.link(engine.tensor_tensor(total, first, values[:, 2 * step:2 * step + 2, :], ALU.add))
            if step < 3:
                return None
            return engine.tensor_tensor(total[:, 0, :], total[:, 0, :], total[:, 1, :], ALU.add)

        def add_squares(engine, e, chain, k, step):
            ins = add_group(engine, e, chain, sq[:, 0:2, :], sq, step, lambda gr: e.wait_ge(sq_ready, 4 * k + gr + 1))
            if ins is not None:
                ins.then_inc(sum_ready, 1)

        def mean_total(k):
            return rows[(k + 1) % 2][:, :].rearrange("p (t n) -> p t n", t=2)

        DOWN_BASE = {U_FF: 0, U_POOL: 3, U_GLU0: 6, U_GLU1: 9}

        @block.sync
        def _(sp):
            for t in range(TT):
                sp.dma_start(x_tok[:, t, :], x[t * P:(t + 1) * P, :]).then_inc(x_landed, 16)
            for n in range(RING):
                sp.dma_start(w32[n][:, :], w_stream[n]).then_inc(w_landed[n], 16)
                if n == 0:
                    sp.dma_start(par[:, :], params).then_inc(par_landed, 16)
            sp.dma_start(con[:, :], consts).then_inc(con_landed, 16)
            sp.dma_start(pos_i[:, :], positions.partition_broadcast(P)).then_inc(pos_landed, 16)
            for rr in range(2):
                first = GRID_ROWS - 3 - rr
                sp.dma_start(bias_na[rr * GRID_W:(rr + 1) * GRID_W, :, :],
                             rpb[:, :, first * GRID_W:(first + BIAS_ROWS) * GRID_W]).then_inc(bias_landed, 16)
            rounds = N_UNITS // RING - 1
            with sp.Fori(0, rounds) as i:
                for s in range(RING):
                    sp.wait_ge(w_lo_ready, s + 1 + RING * i)
                    sp.dma_start(w32[s][:, :], w_stream[bass.ds(RING + s + RING * i, 1), :, :].rearrange("a p n -> p (a n)"))\
                        .then_inc(w_landed[s], 16)
            for n in range(RING * (rounds + 1), N_UNITS):
                sp.wait_ge(w_lo_ready, n - RING + 1)
                sp.dma_start(w32[n % RING][:, :], w_stream[n]).then_inc(w_landed[n % RING], 16)
            for t in range(TT):
                sp.wait_ge(out_act_ready, t + 1)
                sp.wait_ge(out_dve_ready, t + 1)
                sp.dma_start(out[t * P:(t + 1) * P, :], out_tok[:, t, :]).then_inc(out_stored, 16)
            sp.wait_ge(out_stored, 16 * TT)

        @block.gpsimd
        def _(pool):
            chain = Chain(pool, pool_chain)
            g = nc.gpsimd
            g.memset(inv_d[:, :], 1.0 / D)
            g.memset(neg_half[:, :], -0.5)
            g.memset(ident[:, :], 0.0).then_inc(ident_zero, 1)
            pool.wait_ge(ident_zero, 1)
            g.affine_select(out=ident[:, :], in_=ident[:, :], compare_op=ALU.not_equal, fill=1.0, base=0,
                            pattern=[[-1, P]], channel_multiplier=1).then_inc(const_ready, 1)
            pool.wait_ge(ln0_var, 1)
            pool.wait_ge(const_ready, 1)
            g.tensor_tensor(stat[:, S_LN0, 2:4], stat[:, S_LN0, 0:2], neg_half[:, :], ALU.pow).then_inc(ln0_rstd, 1)
            pool.wait_ge(con_landed, 16)
            pool.wait_ge(bias_landed, 16 * 2)
            rows_all = region[:, 0:HEADS_NA * BIAS_W].rearrange("p (r k) -> p r k", k=GRID_W)
            g.tensor_tensor(rows_all, rows_all,
                            ccol("na_mask", 0, GRID_W).unsqueeze(1).to_broadcast([P, HEADS_NA * BIAS_ROWS, GRID_W]),
                            ALU.add).then_inc(bias_ready, 1)

            def residual_plus_bias(bias, fill):
                for c in range(DC):
                    pool.wait_ge(x_ready, DC * fill + c + 1)
                    ins = g.tensor_scalar(res[:, c, :], res[:, c, :], ALPHA, pcol(bias, c), ALU.mult, ALU.add)
                    if c % 2:
                        ins.then_inc(res_b_ready, 1)

            def inverse_root(k, ready):
                pool.wait_ge(ready, k + 1)
                g.tensor_tensor(stat[:, k, 2:4], stat[:, k, 0:2], neg_half[:, :], ALU.pow).then_inc(rstd_ready, 1)

            def shift(k_ln, k):
                for gr in range(2):
                    pool.wait_ge(scaled_ready, 4 * k_ln + gr + 1)
                    g.tensor_tensor(raw[:, 2 * gr:2 * gr + 2, :], raw[:, 2 * gr:2 * gr + 2, :],
                                    twice(rows[k % 2][:, T:2 * T]), ALU.add).then_inc(pool_added, 1)

            def add_residual(index):
                for gr in range(1, 4):
                    pool.wait_ge(scaled_ready, 4 * index + gr + 1)
                    g.tensor_tensor(res[:, 2 * gr:2 * gr + 2, :], res[:, 2 * gr:2 * gr + 2, :],
                                    raw[:, 2 * gr:2 * gr + 2, :], ALU.add).then_inc(pool_added, 1)

            def add_values(k, wait_group):
                for step in range(1, 4):
                    ins = add_group(g, pool, chain, mean_total(k), raw, step, wait_group)
                ins.then_inc(mean_ready, 1)

            def square_sum(k):
                for step in range(1, 4):
                    add_squares(g, pool, chain, k, step)

            def normalise(h, spans):
                pool.wait_ge(rden_ready, h + 1)
                p = probs[h % 2]
                for t, (a, b) in enumerate(spans):
                    ins = g.tensor_scalar(p[:, a:b], p[:, a:b], small[:, 4, 2 * h + t:2 * h + t + 1], 1.0,
                                          ALU.mult, ALU.mult)
                ins.then_inc(pn_ready, 1)

            pool.wait_ge(par_landed, 16)
            residual_plus_bias("b_out", X_LN0)
            for h in range(16):
                normalise(h, [(0, T), (T, 2 * T)])
            add_values(LN1, lambda gr: pool.wait_ge(up_read, UP_INDEX[U_WOUT + gr] + 1))
            inverse_root(LN1, var_ready)
            shift(0, LN1)
            residual_plus_bias("b_ff2", X_LN1)
            add_values(LN2, lambda gr: pool.wait_ge(raw_ready, gr + 1))
            inverse_root(LN2, var_ready)
            shift(1, LN2)
            inverse_root(MIXPRE0, var_ready)
            inverse_root(MIXPOST0, var_ready)
            add_residual(2)
            square_sum(FFNPRE0)
            inverse_root(FFNPRE0, var_ready)

            def glu_products(rounds):
                def product(at, j, j0):
                    pool.wait_ge(gelu_ready, at.pair(j + 1))
                    pool.wait_ge(conv_ready, at.pair(j + 1))
                    if j > j0:
                        pool.wait_ge(mid_ready, PAIRS1 + at.pair(j))
                    g.tensor_tensor(glu_m, glu_g, glu_c[1], ALU.mult).then_inc(mid_f32, 1)
                product(STRAIGHT, rounds, rounds)
                with pool.Fori(0, (PAIRS2 - 1) // 2) as i:
                    at = Looped(i, 4, 2)
                    product(at, rounds + 1, rounds)
                    product(at, rounds + 2, rounds)

            glu_products(0)
            inverse_root(FFNPOST0, var_ready)
            add_residual(3)
            square_sum(MIXPRE1)
            inverse_root(MIXPRE1, var_ready)
            for h in range(16, 32):
                normalise(h, [(0, P), (P, P + T)])
            inverse_root(MIXPOST1, var_ready)
            add_residual(4)
            square_sum(FFNPRE1)
            inverse_root(FFNPRE1, var_ready)
            glu_products(PAIRS2)
            inverse_root(FFNPOST1, var_ready)
            add_residual(5)

        @block.scalar
        def _(act):
            chain = Chain(act, act_chain)
            a = nc.scalar

            def split(at, n):
                s = n % RING
                if n >= RING:
                    act.wait_ge(unit_done, at.unit(n - RING + 1))
                act.wait_ge(w_landed[s], at.landed(n))
                a.activation(w_hi[s][:, :], w32[s][:, :], ACT.Copy).then_inc(w_hi_ready, 1)

            def square(k, gr, src, ready=None, value=0):
                if ready is not None:
                    act.wait_ge(ready, value)
                if k:
                    act.wait_ge(stat_done, k)
                a.activation(sq[:, 2 * gr:2 * gr + 2, :], src, ACT.Square).then_inc(sq_ready, 1)

            def next_split(at, n):
                if n + RING < N_UNITS:
                    split(at, n + RING)

            split(STRAIGHT, 0)
            act.wait_ge(ln0_shift, 1)
            a.activation(xn_tok[:, 0, :], x_tok[:, 0, :], ACT.Identity, bias=stat[:, S_LN0, 4:5],
                         scale=stat[:, S_LN0, 2:3]).then_inc(xn_ready, 1)
            split(STRAIGHT, 1)
            act.wait_ge(par_landed, 16)
            for c in range(DC):
                if c % 2 == 0:
                    act.wait_ge(ln0_turned, c // 2 + 1)
                a.activation(res[:, c, :], down[c // 2][:, (c % 2) * T:(c % 2 + 1) * T], ACT.Identity,
                             bias=pcol("ln0_b", c), scale=pcol("ln0_g", c)).then_inc(ln0_h, 1)
            split(STRAIGHT, 2)
            act.wait_ge(angle_ready, 1)
            a.activation(sin2[:, :], angle[0], ACT.Sin).then_inc(trig_ready, 1)
            act.wait_ge(angle_ready, 2)
            a.activation(cos2[:, :], angle[1], ACT.Sin).then_inc(trig_ready, 1)
            for n in range(U_QKV, U_GATE):
                act.wait_ge(unit_done, n + 1)
                for t in range(2):
                    ins = a.activation(proj[:, 2 * n + t, :], up[n % RING][:, t * T:(t + 1) * T], ACT.Identity,
                                       bias=pcol("b_in", 2 * n + t))
                ins.then_inc(up_read, 1)
                next_split(STRAIGHT, n)

            def exps(h, spans, sink):
                act.wait_ge(negmax_ready, h + 1)
                if h >= 2:
                    act.wait_ge(pt_done, h - 1)
                for t, (lo, hi) in enumerate(spans):
                    ins = a.activation(probs[h % 2][:, lo:hi], scores[h % 2][:, lo:hi], ACT.Exp,
                                       bias=small[:, 0, 2 * h + t:2 * h + t + 1],
                                       accum_out=small[:, 1, 2 * h + t:2 * h + t + 1])
                if sink is not None:
                    ins = a.activation(small[:, 2, 2 * h:2 * h + 2], small[:, 0, 2 * h:2 * h + 2], ACT.Exp, bias=sink)
                ins.then_inc(p_ready, 1)

            def probs_out(h, width):
                act.wait_ge(pt_done, h + 1)
                if h >= 2:
                    act.wait_ge(o_done, h - 1)
                a.activation(probs_t[h % 2][:, 0:width], down[2][:, 0:width], ACT.Copy).then_inc(pt_ready, 1)

            def attention_out(h, fill, chunk):
                act.wait_ge(o_done, h + 1)
                bank = (down[3], aux)[chunk % 2]
                a.activation(x_hi[fill % 2][:, chunk, :], bank[:, 0:T], ACT.Copy).then_inc(x_hi_ready, 1)

            def sink1(h):
                return None if h < 8 else pcol("sink1", h - 8)

            spans1 = [(0, T), (T, 2 * T)]
            exps(0, spans1, None)
            exps(1, spans1, None)
            for h in range(16):
                if h == 0:
                    act.wait_ge(small_ready, 1)
                if h % 2 == 1:
                    n = U_GATE + h // 2
                    act.wait_ge(unit_done, n + 1)
                    for t in range(2):
                        c = 2 * (n - U_GATE) + t
                        ins = a.activation(gates[:, c, :], up[n % RING][:, t * T:(t + 1) * T], ACT.Tanh,
                                           bias=half_gate_bias[:, c:c + 1], scale=0.5)
                    ins.then_inc(up_read, 1)
                probs_out(h, 2 * T)
                if h + 2 < 16:
                    exps(h + 2, spans1, sink1(h + 2))
                if h % 2 == 1:
                    next_split(STRAIGHT, U_GATE + h // 2)
                if h % 2 == 0 and h >= 2:
                    attention_out(h - 1, X_O1, h // 2 - 1)
            attention_out(15, X_O1, 7)

            for half in range(2):
                next_split(STRAIGHT, U_BRANCH + 2 * half)
                for gr in range(2 * half, 2 * half + 2):
                    act.wait_ge(mixed_ready, gr + 1)
                    a.activation(x_hi[X_MIXED % 2][:, 2 * gr:2 * gr + 2, :], raw[:, 2 * gr:2 * gr + 2, :], ACT.Copy,
                                 scale=0.5).then_inc(x_hi_ready, 1)
                next_split(STRAIGHT, U_BRANCH + 2 * half + 1)

            def squares_of_sum(k, index):
                for gr in range(4):
                    square(k, gr, raw[:, 2 * gr:2 * gr + 2, :], raw_ready, 4 * index + gr + 1)

            def squares_of_units(k, units):
                for gr in range(4):
                    if units == U_WO and gr < 3:
                        next_split(STRAIGHT, units + gr)
                    square(k, gr, raw[:, 2 * gr:2 * gr + 2, :], up_read, UP_INDEX[units + gr] + 1)
                    if units != U_WO and gr < 3:
                        next_split(STRAIGHT, units + gr)

            def ln_affine(k_ln, g_name, b_name):
                for gr in range(4):
                    wait_added(act, k_ln, gr)
                    for c in (2 * gr, 2 * gr + 1):
                        ins = a.activation(res[:, c, :], raw[:, c, :], ACT.Identity, bias=pcol(b_name, c),
                                           scale=pcol(g_name, c))
                    ins.then_inc(res_ready, 1)

            squares_of_units(LN1, U_WOUT)
            ln_affine(0, "ln1_g", "ln1_b")
            next_split(STRAIGHT, U_WOUT + 3)

            def relu_square(at, n, j):
                s = n % RING
                act.wait_ge(unit_done, at.unit(n + 1))
                if j:
                    act.wait_ge(mid_ready, at.pair(j))
                for t in range(2):
                    ins = a.activation(relu_v[:, t, :], up[s][:, t * T:(t + 1) * T], ACT.Relu,
                                       bias=pdyn("b_ff1", 2 * at.pair(j) + t))
                ins.then_inc(up_read, 1)
                act.wait_ge(up_read, at.up(UP_INDEX[n] + 1))
                a.activation(mid_hi[j % 3][:, :, :], relu_v, ACT.Square).then_inc(mid_hi_ready, 1)

            def ff_units(at, j):
                relu_square(at, U_FF + 2 * j - 1, j)
                next_split(at, U_FF + 2 * j - 1)
                next_split(at, U_FF + 2 * j)

            relu_square(STRAIGHT, U_FF, 0)
            next_split(STRAIGHT, U_FF)
            for j in range(1, 4):
                ff_units(STRAIGHT, j)
            with act.Fori(0, (PAIRS1 - 4) // 3) as i:
                at = Looped(i, 3, 3)
                for j in range(4, 7):
                    ff_units(at, j)
            squares_of_sum(LN2, 0)
            ln_affine(1, "ln2_g", "ln2_b")
            for gr in range(4):
                square(MIXPRE0, gr, res[:, 2 * gr:2 * gr + 2, :], res_ready, 4 + gr + 1)
            next_split(STRAIGHT, U_FF + 2 * PAIRS1 - 1)

            for gr in range(4):
                act.wait_ge(diff_ready, gr + 1)
                a.activation(x_hi[X_POOL % 2][:, 2 * gr:2 * gr + 2, :], sq[:, 2 * gr:2 * gr + 2, :], ACT.Copy)\
                    .then_inc(x_hi_ready, 1)
            act.wait_ge(x_ready, DC * (X_POOL + 1))
            squares_of_sum(MIXPOST0, 1)
            next_split(STRAIGHT, U_POOL)

            def fill(k, index, fills):
                for gr in range(4):
                    wait_added(act, index, gr)
                    name, which = fills[0]
                    for c in (2 * gr, 2 * gr + 1):
                        a.activation(x_hi[which % 2][:, c, :], res[:, c, :], ACT.Copy, scale=pcol(name, c))\
                            .then_inc(x_hi_ready, 1)
                    square(k, gr, res[:, 2 * gr:2 * gr + 2, :])
                for name, which in fills[1:]:
                    for c in range(DC):
                        a.activation(x_hi[which % 2][:, c, :], res[:, c, :], ACT.Copy, scale=pcol(name, c))\
                            .then_inc(x_hi_ready, 1)

            def glu_pair(at, base, layer, j):
                first = PAIRS2 * layer
                units = (base + 3 * j - 1, base + 3 * j) if j else (base, base + 1)
                for kind in range(2):
                    act.wait_ge(up_read, at.up(UP_INDEX[units[kind]] + 1))
                    if layer or j:
                        act.wait_ge(mid_f32, at.pair(first + j))
                    for t in range(2):
                        col = 16 * at.pair(j) + 8 * kind + 4 * t
                        ins = a.activation(glu_c[kind][:, t, :], glu_u[kind][:, t, 2:T + 2], ACT.Identity,
                                           bias=pdyn(f"conv{layer}", col + 3), scale=pdyn(f"conv{layer}", col + 2))
                    ins.then_inc(conv_first, 1)
                    if kind == 0 and j:
                        next_split(at, units[0])
                act.wait_ge(glu_ready, at.pair(first + j + 1))
                a.activation(glu_g, glu_c[0], ACT.Gelu_apprx_tanh).then_inc(gelu_ready, 1)
                if j < PAIRS2 - 1:
                    next_split(at, units[1])
                act.wait_ge(mid_f32, at.pair(first + j + 1))
                a.activation(mid_hi[j % 2][:, :, :], glu_m, ACT.Copy).then_inc(mid_hi_ready, 1)
                if j == PAIRS2 - 1:
                    next_split(at, units[1])
                if j:
                    next_split(at, base + 3 * j + 1)

            def glu(base, layer):
                next_split(STRAIGHT, base)
                glu_pair(STRAIGHT, base, layer, 0)
                glu_pair(STRAIGHT, base, layer, 1)
                glu_pair(STRAIGHT, base, layer, 2)
                with act.Fori(0, GLU_ROUNDS) as i:
                    at = Looped(i, 4, 2)
                    glu_pair(at, base, layer, 3)
                    glu_pair(at, base, layer, 4)
                for j in range(3 + 2 * GLU_ROUNDS, PAIRS2):
                    glu_pair(STRAIGHT, base, layer, j)

            fill(FFNPRE0, 2, [("ffn_pre0", X_FFN0)])
            glu(U_GLU0, 0)
            squares_of_sum(FFNPOST0, 2)
            next_split(STRAIGHT, U_GLU0 + 3 * PAIRS2 - 1)
            fill(MIXPRE1, 3, [("kv_g", X_KV), ("mix_pre1", X_Q)])

            spans2 = [(0, P), (P, P + T)]

            def sink2(h):
                return pcol("sink2", h)

            next_split(STRAIGHT, U_KV)
            next_split(STRAIGHT, U_KV + 1)
            next_split(STRAIGHT, U_Q)
            exps(16, spans2, sink2(0))
            next_split(STRAIGHT, U_Q + 1)
            exps(17, spans2, sink2(1))
            for h in range(16):
                probs_out(16 + h, P + T)
                if h + 2 < 16:
                    exps(16 + h + 2, spans2, sink2(h + 2))
                if h in (2, 6):
                    next_split(STRAIGHT, U_Q + 2 + h // 4)
                if h % 2 == 0 and h >= 2:
                    attention_out(16 + h - 1, X_O2, h // 2 - 1)
            attention_out(31, X_O2, 7)
            squares_of_units(MIXPOST1, U_WO)
            next_split(STRAIGHT, U_WO + 3)
            fill(FFNPRE1, 4, [("ffn_pre1", X_FFN1)])
            glu(U_GLU1, 1)
            squares_of_sum(FFNPOST1, 3)
            for t in range(TT):
                act.wait_ge(out_turned, 2 * t + 1)
                a.activation(out_tok[:, t, 0:2 * T], down[2 * t][:, :], ACT.Copy).then_inc(out_act_ready, 1)

        @block.tensor
        def _(pe):
            m = nc.tensor.matmul

            def product(out_ap, w_cols, slot, xh, xl, first, last):
                m(out_ap, w_hi[slot][:, w_cols:w_cols + P], xl, start=first, stop=False, skip_group_check=True)
                m(out_ap, w_hi[slot][:, w_cols:w_cols + P], xh, start=False, stop=False, skip_group_check=True)
                return m(out_ap, w_lo[slot][:, w_cols:w_cols + P], xh, start=False, stop=last, skip_group_check=True)

            def tile(at, n, t, fill, chunks_from=None):
                s = n % RING
                if t == 0:
                    pe.wait_ge(w_lo_ready, at.unit(n + 1))
                    if UP_INDEX[n] >= 2:
                        pe.wait_ge(up_read, at.up(UP_INDEX[n] - 1))
                for c in range(DC):
                    if chunks_from is not None and t == 0:
                        pe.wait_ge(x_ready, chunks_from + c + 1)
                    ins = product(up[s][:, t * T:(t + 1) * T], c * UC + t * P, s, x_hi[fill % 2][:, c, :],
                                  x_lo[fill % 2][:, c, :], c == 0, c == DC - 1)
                if t == 1:
                    ins.then_inc(unit_done, 1)

            def unit(at, n, fill, chunks_from=None):
                tile(at, n, 0, fill, chunks_from)
                tile(at, n, 1, fill)

            def sum_unit(at, n, j, slots, first, last):
                s = n % RING
                pe.wait_ge(w_lo_ready, at.unit(n + 1))
                for o in range(DC):
                    for c in range(2):
                        ins = product(down[o // 2][:, (o % 2) * T:(o % 2 + 1) * T], c * D + o * P, s,
                                      mid_hi[j % slots][:, c, :], mid_lo[j % slots][:, c, :],
                                      first and c == 0 and o % 2 == 0, last and c == 1)
                    if last and o % 2 == 1 and o < DC - 1:
                        ins.then_inc(down_done, 1)
                ins.then_inc(unit_done, 1)

            def statistics(k, with_mean):
                if k:
                    pe.wait_ge(rows_ready, k)
                pe.wait_ge(sum_ready, k + 1)
                for t in range(TT):
                    ins = m(aux[:, t:t + 1], sq[:, 0, t * P:(t + 1) * P], inv_d[:, :], start=(t == 0), stop=True,
                            skip_group_check=True)
                if with_mean:
                    pe.wait_ge(mean_ready, k + 1)
                    for t in range(TT):
                        ins = m(aux[:, 2 + t:3 + t], mean_total(k)[:, 0, t * P:(t + 1) * P], inv_d[:, :], start=False,
                                stop=True, skip_group_check=True)
                ins.then_inc(stat_done, 1)

            def spread(k, with_mean):
                pe.wait_ge(rstd_ready, k + 1)
                if with_mean:
                    pe.wait_ge(shift_ready, k + 1)
                for q in range(2 if with_mean else 1):
                    for t in range(TT):
                        ins = m(aux[:, q * T + t * P:q * T + (t + 1) * P],
                                stat[:, k, 2 + 2 * q + t:3 + 2 * q + t].to_broadcast([P, P]), ident[:, :],
                                start=True, stop=True, skip_group_check=True)
                ins.then_inc(rows_done, 1)

            pe.wait_ge(const_ready, 1)
            pe.wait_ge(xn_ready, 2)
            for c in range(DC):
                for t in range(TT):
                    ins = nc.tensor.transpose(down[c // 2][:, (c % 2) * T + t * P:(c % 2) * T + (t + 1) * P],
                                              xn_tok[:, t, c * P:(c + 1) * P], ident[:, :])
                if c % 2:
                    ins.then_inc(ln0_turned, 1)
            for n in range(U_QKV, U_GATE):
                unit(STRAIGHT, n, X_LN0, 0 if n == 0 else None)
            pe.wait_ge(up_read, 6)
            pe.wait_ge(x_ready, DC)
            for tl in range(4):
                for kc in range(TT):
                    col = (tl % 2) * T + kc * P
                    ins = nc.tensor.transpose(down[2 + tl // 2][:, col:col + P], proj[:, 8 + tl, kc * P:(kc + 1) * P],
                                              ident[:, :])
                if tl % 2:
                    ins.then_inc(v_turned, 1)
            pe.wait_ge(con_landed, 16)
            for tl in range(4):
                if tl == 0:
                    pe.wait_ge(up_read, 8)
                ins = m(down[tl // 2][:, (tl % 2) * T:(tl % 2 + 1) * T], ccol("perm1", 0, P), proj[:, 12 + tl, :],
                        start=(tl % 2 == 0), stop=True, skip_group_check=True)
                if tl % 2:
                    ins.then_inc(rot_done, 1)
            pe.wait_ge(up_read, 9)
            m(aux[:, 0:T], ccol("perm1", 0, P), proj[:, 16, :], start=True, stop=True, skip_group_check=True)\
                .then_inc(rot_done, 1)
            for kc in range(TT):
                ins = nc.tensor.transpose(aux[:, T + kc * P:T + (kc + 1) * P], proj[:, 17, kc * P:(kc + 1) * P], ident[:, :])
            ins.then_inc(v_turned, 1)

            def score(h, q_tile, k_tile, half, plan):
                if h >= 2:
                    pe.wait_ge(s_ready, h - 1)
                rows_ = slice(half * HD, (half + 1) * HD)
                for k, (col, t, keys) in enumerate(plan):
                    ins = m(down[h % 2][:, col:col + keys], proj[rows_, q_tile, t * P:(t + 1) * P],
                            proj[rows_, k_tile, 0:keys], start=(k == 0), stop=True, skip_group_check=True)
                ins.then_inc(s_done, 1)

            def turn(h, plan):
                pe.wait_ge(pn_ready, h + 1)
                if h >= 1:
                    pe.wait_ge(pt_ready, h)
                for src, dst in plan:
                    ins = nc.tensor.transpose(down[2][:, dst:dst + P], probs[h % 2][:, src:src + P], ident[:, :])
                ins.then_inc(pt_done, 1)

            def attend(h, step, fill, half, v, plan):
                pe.wait_ge(pt_ready, h + 1)
                if half == 0 and step // 2 >= 2:
                    pe.wait_ge(x_ready, DC * fill + step // 2 - 1)
                bank = (down[3], aux)[(step // 2) % 2]
                for k, (kc, src, width, q0) in enumerate(plan):
                    ins = m(bank[half * HD:(half + 1) * HD, q0:q0 + width], v(kc), probs_t[h % 2][:, src:src + width],
                            start=(k == 0), stop=(k == len(plan) - 1), skip_group_check=True)
                ins.then_inc(o_done, 1)

            full = [(0, 0, T), (T, 1, T)]
            full_turn = [(t * T + kc * P, kc * T + t * P) for kc in range(TT) for t in range(TT)]
            full_attend = [(kc, kc * T, T, 0) for kc in range(TT)]

            def score1(h):
                if h == 0:
                    pe.wait_ge(rot_read, 2)
                if h == 8:
                    pe.wait_ge(rot_ready, 3)
                if h < 8:
                    score(h, h // 2, 4 + h // 2, h % 2, full)
                else:
                    score(h, 12 + (h - 8) // 2, 16, h % 2, full)

            def attend1(h):
                if h == 0:
                    pe.wait_ge(v_ready, 3)
                    pe.wait_ge(rot_read, 3)
                def v(kc):
                    if h < 8:
                        return v_tok[:, kc, h * HD:(h + 1) * HD]
                    return v_tok_swa[:, kc, (h % 2) * HD:(h % 2 + 1) * HD]
                attend(h, h, X_O1, h % 2, v, full_attend)

            score1(0)
            score1(1)
            for h in range(16):
                if h + 2 < 16:
                    score1(h + 2)
                tile(STRAIGHT, U_GATE + h // 2, h % 2, X_LN0)
                if h == 0:
                    pe.wait_ge(v_ready, 2)
                turn(h, full_turn)
                if h:
                    attend1(h - 1)
            attend1(15)
            for q in range(4):
                n = U_BRANCH + q
                s = n % RING
                pe.wait_ge(w_lo_ready, n + 1)
                branch = q % 2
                pe.wait_ge(x_ready, DC * X_O1 + 4 * branch + 4)
                for o in range(4):
                    b = 2 * branch + o // 2
                    if q >= 2 and o % 2 == 0:
                        pe.wait_ge(mixed_ready, o // 2 + 1)
                    for c in range(4):
                        ins = product(down[b][:, (o % 2) * T:(o % 2 + 1) * T], c * 512 + o * P, s,
                                      x_hi[X_O1 % 2][:, 4 * branch + c, :], x_lo[X_O1 % 2][:, 4 * branch + c, :],
                                      c == 0 and o % 2 == 0, c == 3)
                ins.then_inc(unit_done, 1)
            for gr in range(4):
                unit(STRAIGHT, U_WOUT + gr, X_MIXED, DC * X_MIXED if gr == 0 else None)
            statistics(LN1, True)
            spread(LN1, True)
            unit(STRAIGHT, U_FF, X_LN1, DC * X_LN1)

            def ff_units(at, j):
                unit(at, U_FF + 2 * j - 1, X_LN1)
                pe.wait_ge(mid_ready, at.pair(j))
                sum_unit(at, U_FF + 2 * j, j - 1, 3, j == 1, False)

            for j in range(1, 4):
                ff_units(STRAIGHT, j)
            with pe.Fori(0, (PAIRS1 - 4) // 3) as i:
                at = Looped(i, 3, 3)
                for j in range(4, 7):
                    ff_units(at, j)
            pe.wait_ge(mid_ready, PAIRS1)
            sum_unit(STRAIGHT, U_FF + 2 * PAIRS1 - 1, PAIRS1 - 1, 3, False, True)
            statistics(LN2, True)
            spread(LN2, True)
            statistics(MIXPRE0, False)
            spread(MIXPRE0, False)
            n = U_POOL
            pe.wait_ge(w_lo_ready, n + 1)
            for gr in range(4):
                pe.wait_ge(x_ready, DC * X_POOL + 2 * gr + 2)
                for o in range(2):
                    for c in range(2):
                        ins = product(down[gr][:, o * T:(o + 1) * T], gr * 512 + c * 256 + o * P, n % RING,
                                      x_hi[X_POOL % 2][:, 2 * gr + c, :], x_lo[X_POOL % 2][:, 2 * gr + c, :],
                                      c == 0 and o == 0, c == 1)
                if gr < 3:
                    ins.then_inc(down_done, 1)
            ins.then_inc(unit_done, 1)
            statistics(MIXPOST0, False)
            spread(MIXPOST0, False)

            def glu(base, fill, k_pre, k_post):
                layer = (U_GLU0, U_GLU1).index(base)
                unit(STRAIGHT, base, fill, DC * fill)
                tile(STRAIGHT, base + 1, 0, fill)
                statistics(k_pre, False)
                tile(STRAIGHT, base + 1, 1, fill)
                spread(k_pre, False)

                def units(at, j):
                    unit(at, base + 3 * j - 1, fill)
                    unit(at, base + 3 * j, fill)
                    pe.wait_ge(mid_ready, PAIRS1 + PAIRS2 * layer + at.pair(j))
                    sum_unit(at, base + 3 * j + 1, j - 1, 2, j == 1, False)

                for j in range(1, 3):
                    units(STRAIGHT, j)
                with pe.Fori(0, (PAIRS2 - 3) // 2) as i:
                    at = Looped(i, 4, 2)
                    units(at, 3)
                    units(at, 4)
                pe.wait_ge(mid_ready, PAIRS1 + PAIRS2 * (layer + 1))
                sum_unit(STRAIGHT, base + 3 * PAIRS2 - 1, PAIRS2 - 1, 2, False, True)
                statistics(k_post, False)
                spread(k_post, False)

            glu(U_GLU0, X_FFN0, FFNPRE0, FFNPOST0)
            unit(STRAIGHT, U_KV, X_KV, DC * X_KV)
            tile(STRAIGHT, U_KV + 1, 0, X_KV)
            statistics(MIXPRE1, False)
            tile(STRAIGHT, U_KV + 1, 1, X_KV)
            spread(MIXPRE1, False)

            def partners(n, first_tile):
                pe.wait_ge(up_read, UP_INDEX[n] + 1)
                for t in range(2):
                    ins = m(up[n % RING][:, t * T:(t + 1) * T], ccol("perm2", 0, P), proj[:, first_tile + t, :],
                            start=(t == 0), stop=True, skip_group_check=True)
                ins.then_inc(rot_done, 1)

            unit(STRAIGHT, U_Q, X_Q, DC * X_Q)
            partners(U_KV, 0)
            pe.wait_ge(up_read, UP_INDEX[U_KV + 1] + 1)
            for tl in range(2):
                for kc in range(TT):
                    ins = nc.tensor.transpose(down[2][:, tl * T + kc * P:tl * T + (kc + 1) * P],
                                              proj[:, 2 + tl, kc * P:(kc + 1) * P], ident[:, :])
            ins.then_inc(v_turned, 1)
            pe.wait_ge(rot_read, 4)
            unit(STRAIGHT, U_Q + 1, X_Q)
            partners(U_Q, 4)
            partners(U_Q + 1, 6)

            causal = [(0, 0, P), (P, 1, T)]
            causal_turn = [(0, 0), (P, P), (2 * P, 2 * P)]
            causal_attend = [(0, 0, T, 0), (1, T, P, P)]

            def score2(h):
                if h % 4 == 0:
                    pe.wait_ge(rot_ready, 3 + 2 + h // 4)
                score(16 + h, 4 + h // 2, h // 8, h % 2, causal)

            def attend2(h):
                kv = 2 * (h // 8) + h % 2
                attend(16 + h, h, X_O2, h % 2, lambda kc: v_tok2[:, kc, kv * HD:(kv + 1) * HD], causal_attend)

            def out_chunk(u, c):
                n = U_WO + u
                s = n % RING
                if c == 0:
                    pe.wait_ge(w_lo_ready, n + 1)
                    pe.wait_ge(up_read, UP_INDEX[n] - 2)
                    pe.wait_ge(rot_read, 6 + u)
                pe.wait_ge(x_ready, DC * X_O2 + c + 1)
                for t in range(2):
                    ins = product(up[s][:, t * T:(t + 1) * T], c * UC + t * P, s, x_hi[X_O2 % 2][:, c, :],
                                  x_lo[X_O2 % 2][:, c, :], c == 0 and t == 0, c == DC - 1)
                if c == DC - 1:
                    ins.then_inc(unit_done, 1)

            out_left = [(u, c) for u in range(3) for c in range(DC)]

            def out_chunks(h, most):
                for _ in range(most):
                    ready = [(u, c) for u, c in out_left if 2 * c + 4 <= h and h >= (1, 6, 10)[u]
                             and (u, c - 1) not in out_left]
                    if ready:
                        out_left.remove(ready[0])
                        out_chunk(*ready[0])

            score2(0)
            score2(1)
            for h in range(16):
                if h + 2 < 16:
                    score2(h + 2)
                if h % 2 == 0 and h < 8:
                    if h == 4:
                        pe.wait_ge(rot_read, 5)
                    tile(STRAIGHT, U_Q + 2 + h // 4, (h // 2) % 2, X_Q)
                if h in (4, 8):
                    partners(U_Q + 1 + h // 4, 6 + 2 * (h // 4))
                if h == 0:
                    pe.wait_ge(v_ready, 4)
                if h >= 8 or h % 2:
                    out_chunks(h, OUT_MOST)
                turn(16 + h, causal_turn)
                if h:
                    attend2(h - 1)
            attend2(15)
            for u, c in out_left:
                out_chunk(u, c)
            unit(STRAIGHT, U_WO + 3, X_O2)
            statistics(MIXPOST1, False)
            spread(MIXPOST1, False)
            glu(U_GLU1, X_FFN1, FFNPRE1, FFNPOST1)
            for t in range(TT):
                for q in range(2):
                    b = 2 * t + q
                    for c in range(4):
                        if t == 0 and c % 2 == 0:
                            wait_added(pe, 5, 2 * q + c // 2)
                        ins = nc.tensor.transpose(down[b][:, c * P:(c + 1) * P],
                                                  res[:, 4 * q + c, t * P:(t + 1) * P], ident[:, :])
                    ins.then_inc(out_turned, 1)

        @block.vector
        def _(dve):
            v = nc.vector
            chain = Chain(dve, dve_chain)

            def split(at, n):
                s = n % RING
                dve.wait_ge(w_hi_ready, at.unit(n + 1))
                v.tensor_tensor(w_lo[s][:, :], w32[s][:, :], w_hi[s][:, :].bitcast(F32), ALU.subtract)\
                    .then_inc(w_lo_ready, 1)

            def next_split(at, n):
                if n + RING < N_UNITS:
                    split(at, n + RING)

            stats6 = scores[0][:, 0:24].rearrange("p (t s) -> p t s", t=TT)
            mv = scores[0][:, 32:36].rearrange("p (t s) -> p t s", t=TT)
            for t in range(TT):
                dve.wait_ge(x_landed, 16 * TT)
                for q in range(2):
                    ins = v.bn_stats(stats6[:, t, 6 * q:6 * q + 6], x_tok[:, t, q * 512:(q + 1) * 512])
            chain.link(ins)
            for t in range(TT):
                ins = v.bn_aggr(mv[:, t, :], stats6[:, t, :])
            chain.link(ins)
            v.tensor_scalar(stat[:, S_LN0, 0:2], mv[:, :, 1], LN_EPS, None, ALU.add).then_inc(ln0_var, 1)
            dve.wait_ge(ln0_rstd, 1)
            v.scalar_tensor_tensor(out=stat[:, S_LN0, 4:6], in0=mv[:, :, 0], scalar=-1.0, in1=stat[:, S_LN0, 2:4],
                                   op0=ALU.mult, op1=ALU.mult).then_inc(ln0_shift, 1)
            dve.wait_ge(ln0_shift, 1)
            v.tensor_scalar(xn_tok[:, 1, :], x_tok[:, 1, :], stat[:, S_LN0, 3:4], stat[:, S_LN0, 5:6], ALU.mult, ALU.add)\
                .then_inc(xn_ready, 1)
            split(STRAIGHT, 0)
            for c in range(DC):
                dve.wait_ge(ln0_h, c + 1)
                v.tensor_copy(x_hi[0][:, c, :], res[:, c, :]).then_inc(x_hi_ready, 1)
                dve.wait_ge(x_hi_ready, c + 1)
                v.tensor_tensor(x_lo[0][:, c, :], res[:, c, :], x_hi[0][:, c, :].bitcast(F32), ALU.subtract)\
                    .then_inc(x_ready, 1)
            split(STRAIGHT, 1)
            split(STRAIGHT, 2)
            dve.wait_ge(pos_landed, 16)
            dve.wait_ge(con_landed, 16)
            dve.wait_ge(par_landed, 16)
            chain.link(v.tensor_copy(angle[0], pos_i[:, :]))
            chain.link(v.tensor_scalar(angle[0], angle[0], ccol("inv_freq2"), None, ALU.mult))
            chain.link(v.tensor_scalar(angle[1], angle[0], 1.0 / (2 * np.pi), ROUND_MAGIC, ALU.mult, ALU.add))
            chain.link(v.tensor_scalar(angle[1], angle[1], ROUND_MAGIC, None, ALU.subtract))
            for part in TWO_PI_PARTS:
                chain.link(v.scalar_tensor_tensor(out=angle[0], in0=angle[1], scalar=-part, in1=angle[0],
                                                  op0=ALU.mult, op1=ALU.add))
            v.tensor_scalar(angle[0], angle[0], PI_BELOW, -PI_BELOW, ALU.min, ALU.max).then_inc(angle_ready, 1)
            dve.wait_ge(angle_ready, 1)
            chain.link(v.tensor_scalar(angle[2], angle[0], -1.0, None, ALU.mult))
            chain.link(v.tensor_tensor(angle[2], angle[2], angle[0], ALU.max))
            v.tensor_scalar(angle[1], angle[2], -1.0, float(np.pi / 2), ALU.mult, ALU.add).then_inc(angle_ready, 1)
            v.tensor_scalar(half_gate_bias[:, :], pcol("b_in", 18, 16), 0.5, None, ALU.mult)
            v.tensor_scalar(neg_sink1[:, :], pcol("sink1", 0, HEADS_SWA), -1.0, None, ALU.mult)
            v.tensor_scalar(neg_sink2[:, :], pcol("sink2", 0, HEADS_2), -1.0, None, ALU.mult).then_inc(small_ready, 1)
            dve.wait_ge(trig_ready, 2)
            chain.link(v.tensor_scalar(sin2[:, :], sin2[:, :], ccol("sign2"), None, ALU.mult))
            for n in range(U_QKV, U_GATE):
                if n < U_GATE - 1:
                    next_split(STRAIGHT, n)

            def values_out(r, bank, dst, tiles, col=0):
                dve.wait_ge(v_turned, r)
                src = bank[:, col:col + tiles * T].rearrange("p (a k c) -> p a k c", a=tiles, k=TT)
                v.tensor_copy(dst, src).then_inc(v_ready, 1)

            def rotate(r, bank, tiles, count, cos, sin):
                dve.wait_ge(rot_done, r)
                src = bank[:, 0:count * T].rearrange("p (t n) -> p t n", t=count)
                t_ = tmp_rot[r % 2][:, 0:count, :]
                v.tensor_tensor(t_, src, sin.unsqueeze(1).to_broadcast([P, count, T]), ALU.mult).then_inc(rot_read, 1)
                chain.link(v.tensor_tensor(proj[:, tiles:tiles + count, :], proj[:, tiles:tiles + count, :],
                                           cos.unsqueeze(1).to_broadcast([P, count, T]), ALU.mult))
                dve.wait_ge(rot_read, r)
                v.tensor_tensor(proj[:, tiles:tiles + count, :], proj[:, tiles:tiles + count, :], t_, ALU.add)\
                    .then_inc(rot_ready, 1)

            def v_dst(buf, first, tiles):
                return buf[:, :, first * P:(first + tiles) * P].rearrange("p k (a c) -> p a k c", a=tiles)

            values_out(1, down[2], v_dst(v_tok, 0, 2), 2)
            values_out(2, down[3], v_dst(v_tok, 2, 2), 2)
            for r in range(1, 4):
                if r == 3:
                    values_out(3, aux, v_dst(v_tok_swa, 0, 1), 1, col=T)
                bank, tiles, count = ((down[0], 12, 2), (down[1], 14, 2), (aux, 16, 1))[r - 1]
                rotate(r, bank, tiles, count, ccol("cos1", 0, T), ccol("sin1", 0, T))
            next_split(STRAIGHT, U_GATE - 1)

            def scores_out(h, bias, spans, neg_sink, width):
                dve.wait_ge(s_done, h + 1)
                if h >= 2:
                    dve.wait_ge(p_ready, h - 1)
                dst, src = scores[h % 2][:, 0:width], down[h % 2][:, 0:width]
                if width == 2 * T:
                    dst, src = pair_view(dst), pair_view(src)
                v.scalar_tensor_tensor(out=dst, in0=src, scalar=SCALE, in1=bias, op0=ALU.mult, op1=ALU.add)\
                    .then_inc(s_ready, 1)
                dve.wait_ge(s_ready, h + 1)
                if width == 2 * T:
                    ins = v.tensor_reduce(small[:, 0, 2 * h:2 * h + 2], dst, AX_X, ALU.max, negate=True)
                else:
                    for t, (lo, hi) in enumerate(spans):
                        ins = v.tensor_reduce(small[:, 0, 2 * h + t:2 * h + t + 1], scores[h % 2][:, lo:hi], AX_X,
                                              ALU.max, negate=True)
                if neg_sink is not None:
                    chain.link(ins)
                    ins = v.tensor_scalar(small[:, 0, 2 * h:2 * h + 2], small[:, 0, 2 * h:2 * h + 2], neg_sink, None,
                                          ALU.min)
                ins.then_inc(negmax_ready, 1)

            def denominators(h, with_sink):
                dve.wait_ge(p_ready, h + 1)
                src = small[:, 1, 2 * h:2 * h + 2]
                if with_sink:
                    chain.link(v.tensor_tensor(small[:, 3, 2 * h:2 * h + 2], src, small[:, 2, 2 * h:2 * h + 2], ALU.add))
                    src = small[:, 3, 2 * h:2 * h + 2]
                v.reciprocal(small[:, 4, 2 * h:2 * h + 2], src).then_inc(rden_ready, 1)

            def attention_out(fill, chunk):
                dve.wait_ge(x_hi_ready, hi_count[fill] + chunk + 1)
                bank = (down[3], aux)[chunk % 2]
                v.tensor_tensor(x_lo[fill % 2][:, chunk, :], bank[:, 0:T], x_hi[fill % 2][:, chunk, :].bitcast(F32),
                                ALU.subtract).then_inc(x_ready, 1)

            hi_count, at_ = {}, 0
            for f in range(10):
                hi_count[f] = at_
                at_ += 4 if f in (X_MIXED, X_LN1, X_POOL) else DC

            spans1 = [(0, T), (T, 2 * T)]

            def scores1(h):
                if h == 0:
                    dve.wait_ge(bias_ready, 1)
                    dve.wait_ge(small_ready, 1)
                if h < 8:
                    scores_out(h, shifted(region, REGION, h * BIAS_W), spans1, None, 2 * T)
                else:
                    scores_out(h, shifted(con, N_CON, CON["swa_mask"]), spans1, neg_sink1[:, h - 8:h - 7], 2 * T)

            scores1(0)
            scores1(1)
            denominators(0, False)
            denominators(1, False)
            for h in range(16):
                if h + 2 < 16:
                    scores1(h + 2)
                if h % 2 == 0 and h >= 2:
                    attention_out(X_O1, h // 2 - 1)
                    next_split(STRAIGHT, U_GATE + h // 2 - 1)
                if h + 2 < 16:
                    denominators(h + 2, h + 2 >= 8)
            next_split(STRAIGHT, U_GATE + 7)
            attention_out(X_O1, 7)

            for half in range(2):
                next_split(STRAIGHT, U_BRANCH + 2 * half)
                dve.wait_ge(unit_done, U_BRANCH + 2 * half + 2)
                for q in range(2):
                    gr = 2 * half + q
                    v.scalar_tensor_tensor(out=pair_view(scores[q][:, :]), in0=gates[:, 2 * gr:2 * gr + 2, :], scalar=1.0,
                                           in1=pair_view(down[q][:, :]), op0=ALU.add, op1=ALU.mult)
                    chain.link(v.scalar_tensor_tensor(out=raw[:, 2 * gr:2 * gr + 2, :],
                                                      in0=gates[:, DC + 2 * gr:DC + 2 * gr + 2, :], scalar=1.0,
                                                      in1=pair_view(down[2 + q][:, :]), op0=ALU.add, op1=ALU.mult))
                    v.tensor_tensor(raw[:, 2 * gr:2 * gr + 2, :], raw[:, 2 * gr:2 * gr + 2, :], pair_view(scores[q][:, :]),
                                    ALU.add).then_inc(mixed_ready, 1)
                for q in range(2):
                    gr = 2 * half + q
                    dve.wait_ge(x_hi_ready, hi_count[X_MIXED] + gr + 1)
                    v.scalar_tensor_tensor(out=x_lo[X_MIXED % 2][:, 2 * gr:2 * gr + 2, :],
                                           in0=raw[:, 2 * gr:2 * gr + 2, :], scalar=0.5,
                                           in1=x_hi[X_MIXED % 2][:, 2 * gr:2 * gr + 2, :].bitcast(F32),
                                           op0=ALU.mult, op1=ALU.subtract).then_inc(x_ready, 2)
                next_split(STRAIGHT, U_BRANCH + 2 * half + 1)

            def norm_rows(k, with_mean, eps):
                dve.wait_ge(stat_done, k + 1)
                if with_mean:
                    chain.link(v.tensor_copy(stat[:, k, 6:8], aux[:, 2:4]))
                    chain.link(v.tensor_tensor(stat[:, k, 4:6], stat[:, k, 6:8], stat[:, k, 6:8], ALU.mult))
                    chain.link(v.scalar_tensor_tensor(out=stat[:, k, 0:2], in0=stat[:, k, 4:6], scalar=-1.0,
                                                      in1=aux[:, 0:2], op0=ALU.mult, op1=ALU.add))
                    v.tensor_scalar(stat[:, k, 0:2], stat[:, k, 0:2], 0.0, eps, ALU.max, ALU.add).then_inc(var_ready, 1)
                    dve.wait_ge(rstd_ready, k + 1)
                    v.scalar_tensor_tensor(out=stat[:, k, 4:6], in0=stat[:, k, 6:8], scalar=-1.0,
                                           in1=stat[:, k, 2:4], op0=ALU.mult, op1=ALU.mult).then_inc(shift_ready, 1)
                else:
                    v.tensor_scalar(stat[:, k, 0:2], aux[:, 0:2], eps, None, ALU.add).then_inc(var_ready, 1)
                width = 2 * T if with_mean else T
                dve.wait_ge(rows_done, k + 1)
                v.tensor_copy(rows[k % 2][:, 0:width], aux[:, 0:width]).then_inc(rows_ready, 1)
                dve.wait_ge(rows_ready, k + 1)

            def ln_scale(k, k_ln):
                for gr in range(4):
                    v.tensor_tensor(raw[:, 2 * gr:2 * gr + 2, :], raw[:, 2 * gr:2 * gr + 2, :],
                                    twice(rows[k % 2][:, 0:T]), ALU.mult).then_inc(scaled_ready, 1)
                for gr in range(2, 4):
                    dve.wait_ge(scaled_ready, 4 * k_ln + gr + 1)
                    v.tensor_tensor(raw[:, 2 * gr:2 * gr + 2, :], raw[:, 2 * gr:2 * gr + 2, :],
                                    twice(rows[k % 2][:, T:2 * T]), ALU.add).then_inc(dve_added, 1)

            def square_sum(k):
                for step in range(1, 4):
                    add_squares(v, dve, chain, k, step)

            def post_scale(k, g_name, index):
                for c in range(DC):
                    ins = v.scalar_tensor_tensor(out=raw[:, c, :], in0=raw[:, c, :], scalar=pcol(g_name, c),
                                                 in1=rows[k % 2][:, 0:T], op0=ALU.mult, op1=ALU.mult)
                    if c % 2:
                        ins.then_inc(scaled_ready, 1)
                    if c == 3:
                        dve.wait_ge(scaled_ready, 4 * index + 1)
                        v.tensor_tensor(res[:, 0:2, :], res[:, 0:2, :], raw[:, 0:2, :], ALU.add).then_inc(dve_added, 1)

            def lower(fills):
                for name, which in fills:
                    for c in range(DC):
                        dve.wait_ge(x_hi_ready, hi_count[which] + c + 1)
                        v.scalar_tensor_tensor(out=x_lo[which % 2][:, c, :], in0=res[:, c, :], scalar=pcol(name, c),
                                               in1=x_hi[which % 2][:, c, :].bitcast(F32), op0=ALU.mult,
                                               op1=ALU.subtract).then_inc(x_ready, 1)

            for gr in range(4):
                n = U_WOUT + gr
                dve.wait_ge(unit_done, n + 1)
                dve.wait_ge(res_b_ready, 4)
                v.tensor_tensor(raw[:, 2 * gr:2 * gr + 2, :], pair_view(up[n % RING][:, :]),
                                res[:, 2 * gr:2 * gr + 2, :], ALU.add).then_inc(up_read, 1)
                if gr < 3:
                    next_split(STRAIGHT, n)
                if gr >= 2:
                    add_squares(v, dve, chain, LN1, gr - 1)
            add_squares(v, dve, chain, LN1, 3)
            norm_rows(LN1, True, LN_EPS)
            ln_scale(LN1, 0)
            for gr in range(4):
                dve.wait_ge(res_ready, gr + 1)
                v.tensor_copy(x_hi[X_LN1 % 2][:, 2 * gr:2 * gr + 2, :], res[:, 2 * gr:2 * gr + 2, :])\
                    .then_inc(x_hi_ready, 1)
                dve.wait_ge(x_hi_ready, hi_count[X_LN1] + gr + 1)
                v.tensor_tensor(x_lo[X_LN1 % 2][:, 2 * gr:2 * gr + 2, :], res[:, 2 * gr:2 * gr + 2, :],
                                x_hi[X_LN1 % 2][:, 2 * gr:2 * gr + 2, :].bitcast(F32), ALU.subtract)\
                    .then_inc(x_ready, 2)
            next_split(STRAIGHT, U_WOUT + 3)

            def relu_square(at, n, j):
                dve.wait_ge(mid_hi_ready, at.pair(j + 1))
                s = j % 3
                chain.link(v.tensor_tensor(relu_v, relu_v, relu_v, ALU.mult))
                v.tensor_tensor(mid_lo[s][:, :, :], relu_v, mid_hi[s][:, :, :].bitcast(F32), ALU.subtract)\
                    .then_inc(mid_ready, 1)

            def ff_units(at, j):
                relu_square(at, U_FF + 2 * j - 1, j)
                next_split(at, U_FF + 2 * j - 1)
                next_split(at, U_FF + 2 * j)

            relu_square(STRAIGHT, U_FF, 0)
            next_split(STRAIGHT, U_FF)
            for j in range(1, 4):
                ff_units(STRAIGHT, j)
            with dve.Fori(0, (PAIRS1 - 4) // 3) as i:
                at = Looped(i, 3, 3)
                chain.enter(i, 3)
                for j in range(4, 7):
                    ff_units(at, j)
            chain.leave((PAIRS1 - 4) // 3)

            def sums_out(base, n_last, how, k):
                for gr in range(4):
                    if gr < 3:
                        dve.wait_ge(down_done, DOWN_BASE[base] + gr + 1)
                    else:
                        dve.wait_ge(unit_done, n_last + 1)
                    how(gr).then_inc(raw_ready, 1)
                    if gr >= 2:
                        add_squares(v, dve, chain, k, gr - 1)
                add_squares(v, dve, chain, k, 3)

            dve.wait_ge(res_b_ready, 8)
            sums_out(U_FF, U_FF + 2 * PAIRS1 - 1,
                     lambda gr: v.tensor_tensor(raw[:, 2 * gr:2 * gr + 2, :], pair_view(down[gr][:, :]),
                                                res[:, 2 * gr:2 * gr + 2, :], ALU.add), LN2)
            norm_rows(LN2, True, LN_EPS)
            ln_scale(LN2, 1)
            for k in range(2):
                v.memset(glu_u[k][:, :, 0:2], 0.0)
            chain.link(v.memset(pooled[:, :, 0:PAD], 0.0))
            square_sum(MIXPRE0)
            norm_rows(MIXPRE0, False, RMS_EPS)
            for c in range(DC):
                ins = v.scalar_tensor_tensor(out=pooled[:, c, PAD:], in0=res[:, c, :], scalar=pcol("mix_pre0", c),
                                             in1=rows[MIXPRE0 % 2][:, 0:T], op0=ALU.mult, op1=ALU.mult)
            chain.link(ins)
            for gr, window in enumerate(POOL_WINDOWS):
                if gr:
                    dve.wait_ge(diff_ready, gr)
                src, start = pooled[:, 2 * gr:2 * gr + 2, :], 0
                width = 1
                while width < window:
                    dst = run_b if (width in (1, 4)) else run_a
                    lo = start + width
                    chain.link(v.tensor_tensor(dst[:, :, lo:], src[:, :, lo:], src[:, :, start:T + PAD - width], ALU.add))
                    src, start = dst, lo
                    width *= 2
                chain.link(v.tensor_tensor(src[:, :, PAD:2 * PAD], src[:, :, PAD:2 * PAD],
                                           ccol("pool_fix", gr * PAD, PAD).unsqueeze(1).to_broadcast([P, 2, PAD]),
                                           ALU.mult))
                v.scalar_tensor_tensor(out=sq[:, 2 * gr:2 * gr + 2, :], in0=src[:, :, PAD:], scalar=1.0 / window,
                                       in1=pooled[:, 2 * gr:2 * gr + 2, PAD:], op0=ALU.mult, op1=ALU.subtract)\
                    .then_inc(diff_ready, 1)
            for gr in range(4):
                dve.wait_ge(x_hi_ready, hi_count[X_POOL] + gr + 1)
                v.tensor_tensor(x_lo[X_POOL % 2][:, 2 * gr:2 * gr + 2, :], sq[:, 2 * gr:2 * gr + 2, :],
                                x_hi[X_POOL % 2][:, 2 * gr:2 * gr + 2, :].bitcast(F32), ALU.subtract)\
                    .then_inc(x_ready, 2)

            next_split(STRAIGHT, U_FF + 2 * PAIRS1 - 1)

            def pool_scaled(gr):
                for c in (2 * gr, 2 * gr + 1):
                    ins = v.tensor_scalar(raw[:, c, :], down[gr][:, (c % 2) * T:(c % 2 + 1) * T],
                                          pcol("pool_scale", c), None, ALU.mult)
                return ins

            sums_out(U_POOL, U_POOL, pool_scaled, MIXPOST0)
            norm_rows(MIXPOST0, False, RMS_EPS)
            post_scale(MIXPOST0, "mix_post0", 2)
            lower([("ffn_pre0", X_FFN0)])
            next_split(STRAIGHT, U_POOL)

            def glu_pair(at, base, layer, j, k_pre):
                first = PAIRS2 * layer
                units = [base + (3 * j - 1 if j else 0), base + (3 * j if j else 1)]
                for kind in range(2):
                    n = units[kind]
                    dve.wait_ge(unit_done, at.unit(n + 1))
                    v.tensor_tensor(glu_u[kind][:, :, 2:T + 2], pair_view(up[n % RING][:, :]),
                                    twice(rows[k_pre % 2][:, 0:T]), ALU.mult).then_inc(up_read, 1)
                    if kind == 0 and j >= 2:
                        next_split(at, base + 3 * (j - 1) + 1)
                    if kind == 1:
                        if j:
                            next_split(at, units[0])
                    dve.wait_ge(conv_first, 2 * at.pair(first + j) + kind + 1)
                    dve.wait_ge(up_read, at.up(UP_INDEX[n] + 1))
                    for tap in (1, 0):
                        for t in range(2):
                            col = 16 * at.pair(j) + 8 * kind + 4 * t
                            ins = v.scalar_tensor_tensor(out=glu_c[kind][:, t, :], in0=glu_u[kind][:, t, tap:T + tap],
                                                         scalar=pdyn(f"conv{layer}", col + tap),
                                                         in1=glu_c[kind][:, t, :], op0=ALU.mult, op1=ALU.add)
                        if tap:
                            chain.link(ins)
                    ins.then_inc((glu_ready, conv_ready)[kind], 1)
                if j < PAIRS2 - 1:
                    next_split(at, units[1])
                dve.wait_ge(mid_hi_ready, PAIRS1 + at.pair(first + j + 1))
                v.tensor_tensor(mid_lo[j % 2][:, :, :], glu_m, mid_hi[j % 2][:, :, :].bitcast(F32), ALU.subtract)\
                    .then_inc(mid_ready, 1)
                if j == PAIRS2 - 1:
                    next_split(at, units[1])
                    next_split(at, base + 3 * j + 1)

            def glu(base, layer, k_pre, k_post):
                next_split(STRAIGHT, base)
                norm_rows(k_pre, False, RMS_EPS)
                for j in range(3):
                    glu_pair(STRAIGHT, base, layer, j, k_pre)
                with dve.Fori(0, GLU_ROUNDS) as i:
                    at = Looped(i, 4, 2)
                    chain.enter(i, 4)
                    glu_pair(at, base, layer, 3, k_pre)
                    glu_pair(at, base, layer, 4, k_pre)
                chain.leave(GLU_ROUNDS)
                for j in range(3 + 2 * GLU_ROUNDS, PAIRS2):
                    glu_pair(STRAIGHT, base, layer, j, k_pre)
                sums_out(base, base + 3 * PAIRS2 - 1,
                         lambda gr: v.tensor_copy(raw[:, 2 * gr:2 * gr + 2, :], pair_view(down[gr][:, :])), k_post)
                norm_rows(k_post, False, RMS_EPS)

            glu(U_GLU0, 0, FFNPRE0, FFNPOST0)
            post_scale(FFNPOST0, "ffn_post0", 3)
            lower([("kv_g", X_KV), ("mix_pre1", X_Q)])
            next_split(STRAIGHT, U_GLU0 + 3 * PAIRS2 - 1)
            next_split(STRAIGHT, U_KV)
            norm_rows(MIXPRE1, False, RMS_EPS)

            def projected(n, tiles):
                dve.wait_ge(unit_done, n + 1)
                v.tensor_tensor(proj[:, tiles:tiles + 2, :], pair_view(up[n % RING][:, :]),
                                twice(rows[MIXPRE1 % 2][:, 0:T]), ALU.mult).then_inc(up_read, 1)
                dve.wait_ge(up_read, UP_INDEX[n] + 1)

            projected(U_KV, 0)
            projected(U_KV + 1, 2)
            next_split(STRAIGHT, U_KV + 1)
            projected(U_Q, 4)
            rotate(4, up[U_KV % RING], 0, 2, cos2[:, :], sin2[:, :])
            values_out(4, down[2], v_dst(v_tok2, 0, 2), 2)
            next_split(STRAIGHT, U_Q)
            projected(U_Q + 1, 6)
            rotate(5, up[U_Q % RING], 4, 2, cos2[:, :], sin2[:, :])
            rotate(6, up[(U_Q + 1) % RING], 6, 2, cos2[:, :], sin2[:, :])
            spans2 = [(0, P), (P, P + T)]

            def scores2(h):
                scores_out(16 + h, ccol("mask2", 0, P + T), spans2, neg_sink2[:, h:h + 1], P + T)

            scores2(0)
            scores2(1)
            denominators(16, True)
            next_split(STRAIGHT, U_Q + 1)
            for h in range(16):
                if h + 1 < 16:
                    denominators(16 + h + 1, True)
                if h + 2 < 16:
                    scores2(h + 2)
                if h in (4, 8):
                    rotate(6 + h // 4, up[(U_Q + 1 + h // 4) % RING], 6 + 2 * (h // 4), 2, cos2[:, :], sin2[:, :])
                if h in (2, 6):
                    projected(U_Q + 2 + h // 4, 8 + 2 * (h // 4))
                    next_split(STRAIGHT, U_Q + 2 + h // 4)
                if h % 2 == 0 and h >= 2:
                    attention_out(X_O2, h // 2 - 1)
            attention_out(X_O2, 7)
            for gr in range(4):
                n = U_WO + gr
                dve.wait_ge(unit_done, n + 1)
                v.tensor_copy(raw[:, 2 * gr:2 * gr + 2, :], pair_view(up[n % RING][:, :])).then_inc(up_read, 1)
                if gr < 3:
                    next_split(STRAIGHT, n)
                if gr >= 2:
                    add_squares(v, dve, chain, MIXPOST1, gr - 1)
            add_squares(v, dve, chain, MIXPOST1, 3)
            norm_rows(MIXPOST1, False, RMS_EPS)
            post_scale(MIXPOST1, "mix_post1", 4)
            lower([("ffn_pre1", X_FFN1)])
            next_split(STRAIGHT, U_WO + 3)
            glu(U_GLU1, 1, FFNPRE1, FFNPOST1)
            post_scale(FFNPOST1, "ffn_post1", 5)
            for t in range(TT):
                dve.wait_ge(out_turned, 2 * t + 2)
                v.tensor_copy(out_tok[:, t, 2 * T:4 * T], down[2 * t + 1][:, :]).then_inc(out_dve_ready, 1)


def per_partition(vec):
    return vec.reshape(-1, P).T


def head_columns(order):
    return np.concatenate([np.arange(h * HD, (h + 1) * HD) for h in order])


def weight_stream(i):
    def columns(w):
        n = w.shape[1] // UC
        return w.reshape(DC, P, n, UC).transpose(2, 1, 0, 3).reshape(n, P, UNIT)

    def row_pairs(w):
        n = w.shape[0] // (2 * P)
        return w.reshape(n, 2, P, D).transpose(0, 2, 1, 3).reshape(n, P, UNIT)

    def interleave(first, rows):
        out = list(first[0])
        for j in range(1, len(first)):
            out += [*first[j], rows[j - 1]]
        return out + [rows[len(first) - 1]]

    w_in = i["w_in"][0]
    q_b = 3 * 512
    w_in = np.concatenate([w_in[:, :q_b], w_in[:, q_b:q_b + 512][:, head_columns(SWA_ORDER)], w_in[:, q_b + 512:]], axis=1)
    units = list(columns(w_in))
    swa = i["w_branch_swa"][0][head_columns(SWA_ORDER)]
    for half in range(2):
        for w in (i["w_branch_na"][0], swa):
            units.append(w[:, half * 512:(half + 1) * 512].reshape(4, P, 512).transpose(1, 0, 2).reshape(P, UNIT))
    units += list(columns(i["w_out"][0]))
    units += interleave([[u] for u in columns(i["w_ff1"][0])], row_pairs(i["w_ff2"][0]))
    units.append(i["pool_w_2"][0].reshape(4, 2, P, 256).transpose(2, 0, 1, 3).reshape(P, UNIT))

    def glu(layer):
        w = i["ffn_w_in_2"][layer]
        return interleave(list(zip(columns(w[:, :F2]), columns(w[:, F2:]))), row_pairs(i["ffn_w_out_2"][layer]))

    units += glu(0)
    units += list(columns(i["w_kv_2"]))
    units += list(columns(i["w_q_2"][0][:, head_columns(ORDER_2)]))
    units += list(columns(i["w_o_2"][0][head_columns(ORDER_2)]))
    units += glu(1)
    return np.ascontiguousarray(np.stack(units))


def parameters(i):
    b_in = i["b_in"][0]
    q_b = 3 * 512
    b_in = np.concatenate([b_in[:q_b], b_in[q_b:q_b + 512][head_columns(SWA_ORDER)], b_in[q_b + 512:]])

    def conv(layer):
        rows = np.concatenate([i["ffn_conv_w_2"][layer], i["ffn_conv_b_2"][layer][None]])
        return rows.reshape(4, 2, PAIRS2, 2, P).transpose(4, 2, 1, 3, 0).reshape(P, 16 * PAIRS2)

    cols = {
        "ln0_g": i["ln0_g"], "ln0_b": i["ln0_b"], "b_in": b_in, "b_out": i["b_out"][0], "ln1_g": i["ln1_g"][0],
        "ln1_b": i["ln1_b"][0], "b_ff1": i["b_ff1"][0], "b_ff2": i["b_ff2"][0], "ln2_g": i["ln2_g"][0],
        "ln2_b": i["ln2_b"][0], "mix_pre0": i["mix_pre_g_2"][0], "mix_pre1": i["mix_pre_g_2"][1],
        "mix_post0": i["mix_post_g_2"][0], "mix_post1": i["mix_post_g_2"][1], "pool_scale": i["pool_scale_2"][0],
        "kv_g": i["kv_norm_g_2"], "ffn_pre0": i["ffn_pre_g_2"][0], "ffn_pre1": i["ffn_pre_g_2"][1],
        "ffn_post0": i["ffn_post_g_2"][0], "ffn_post1": i["ffn_post_g_2"][1],
    }
    blocks = {k: per_partition(v) for k, v in cols.items()}
    blocks["conv0"], blocks["conv1"] = conv(0), conv(1)
    blocks["sink1"] = np.broadcast_to(i["swa_sink"][0][SWA_ORDER], (P, HEADS_SWA))
    blocks["sink2"] = np.broadcast_to(i["sinks_2"][0][ORDER_2], (P, HEADS_2))
    return np.ascontiguousarray(np.concatenate([blocks[name] for name, _ in PARAM_WIDTHS], axis=1))


def shape_constants():
    p = np.arange(P)[:, None]
    masked = lambda ok: np.where(ok, 0.0, MASKED)
    c, ck = p % GRID_W, np.arange(GRID_W)[None]
    start = np.clip(c - KW // 2, 0, GRID_W - KW)
    j = np.arange(P + T)[None] - P
    k2 = np.concatenate([np.arange(P), np.arange(T) - P])[None]
    d = p % HD
    half = HD // 8
    inv1 = np.power(np.float32(500000.0), -(np.arange(0, 2 * half, 2, dtype=np.float32)) / np.float32(2 * half))
    ang = np.arange(T, dtype=np.float32)[None] * inv1.astype(np.float32)[d % half]
    ang = np.where(d < 2 * half, ang.astype(np.float32).reshape(P, T), np.float32(0)).astype(np.float64)
    partner1 = np.where(d < half, p + half, np.where(d < 2 * half, p - half, p))[:, 0]
    partner2 = np.where(d < HD // 2, p + HD // 2, p - HD // 2)[:, 0]
    eye = np.eye(P)
    inv2 = (1.0 / np.power(np.float32(10000.0), np.arange(0, HD, 2, dtype=np.float32) / np.float32(HD))).astype(np.float32)
    t16 = np.arange(PAD)
    fix = np.concatenate([w / np.minimum(t16 + 1, w) for w in POOL_WINDOWS])
    table = {
        "na_mask": masked((ck >= start) & (ck < start + KW)),
        "swa_mask": masked(np.abs(j - p) <= 128),
        "mask2": masked((p - k2 >= 0) & (p - k2 < 128)),
        "cos1": np.cos(ang), "sin1": np.sin(ang) * np.where(d < half, -1.0, 1.0),
        "perm1": eye[partner1].T, "perm2": eye[partner2].T,
        "pool_fix": np.broadcast_to(fix, (P, 4 * PAD)),
        "inv_freq2": inv2[d[:, 0] % (HD // 2)][:, None], "sign2": np.where(d < HD // 2, -1.0, 1.0),
    }
    return np.ascontiguousarray(np.concatenate([table[name] for name, _ in CONST_WIDTHS], axis=1).astype(np.float32))


def rpb_windows(rpb):
    out = np.zeros((HEADS_NA, 2 * GRID_ROWS - 1, 2 * GRID_W - 1), rpb.dtype)
    first = rpb.shape[1] // 2 - (GRID_ROWS - 1)
    out[:, :, GRID_W - KW:GRID_W - KW + rpb.shape[2]] = rpb[:, first:first + 2 * GRID_ROWS - 1]
    return np.stack([out[:, :, GRID_W - 1 - c:2 * GRID_W - 1 - c].reshape(HEADS_NA, -1) for c in range(GRID_W)])


def kernel(**inputs):
    import concourse.bacc as bacc
    from concourse.bass_utils import run_bass_kernel_spmd

    i = {k: np.asarray(v) for k, v in inputs.items()}
    arrays = {
        "x_in": np.ascontiguousarray(i["x"][0]),
        "w_stream": weight_stream(i),
        "params": parameters(i),
        "consts": shape_constants(),
        "rpb": rpb_windows(i["na_rpb"][0]),
        "positions": np.ascontiguousarray(i["positions_2"][0]),
    }
    nc = bacc.Bacc("TRN2", target_bir_lowering=False, num_devices=1)
    args = [nc.dram_tensor(k, a.shape, mybir.dt.from_np(a.dtype), kind="ExternalInput").ap() for k, a in arrays.items()]
    out = nc.dram_tensor("result", (T, D), F32, kind="ExternalOutput").ap()
    build(nc, *args, out)
    r = run_bass_kernel_spmd(nc, [arrays], core_ids=[0])
    return r.results[0]["result"].reshape(1, T, D)
```

```python
from contextlib import ExitStack

import numpy as np

import concourse.bass as bass
from concourse import mybir

F32 = mybir.dt.float32
F32R = mybir.dt.float32r
I32 = mybir.dt.int32
ALU = mybir.AluOpType
ACT = mybir.ActivationFunctionType
AX_X = mybir.AxisListType.X

P = 128
T = 256
TT = T // P
D = 1024
DC = D // P
HD = 64
HEADS_NA = 8
HEADS_SWA = 8
HEADS_2 = 16
GRID_W = 64
GRID_ROWS = T // GRID_W
KW = 16
F1 = 4096
F2 = 2816
ALPHA = float(2.0 ** 0.25)
LN_EPS = 1e-5
RMS_EPS = 1e-6
MASKED = -1e30
SCALE = float(HD) ** -0.5
POOL_WINDOWS = (2, 4, 8, 16)
BAND0 = P + POOL_WINDOWS[-1]
BAND_W = BAND0 + P

UNIT = 2048
UC = UNIT // DC
RING = 3
U_QKV = 0
U_GATE = U_QKV + 9
U_BRANCH = U_GATE + 8
U_WOUT = U_BRANCH + 4
U_FF = U_WOUT + 4
PAIRS1 = F1 // (2 * P)
U_POOL = U_FF + 2 * PAIRS1
U_GLU0 = U_POOL + 1
PAIRS2 = F2 // (2 * P)
U_KV = U_GLU0 + 3 * PAIRS2
U_Q = U_KV + 2
U_WO = U_Q + 4
U_GLU1 = U_WO + 4
N_UNITS = U_GLU1 + 3 * PAIRS2


def output_tile_units():
    units = list(range(U_QKV, U_BRANCH)) + list(range(U_WOUT, U_FF))
    units += [U_FF] + [U_FF + 1 + 2 * j for j in range(PAIRS1 - 1)]
    for base in (U_GLU0, U_GLU1):
        units += [base, base + 1]
        units += [base + 2 + 3 * j + k for j in range(PAIRS2 - 1) for k in (0, 1)]
    units += list(range(U_KV, U_GLU1))
    return sorted(units)


UP_INDEX = {n: q for q, n in enumerate(output_tile_units())}


def reads_before(n):
    return max([UP_INDEX[m] + 1 for m in UP_INDEX if m < n and m % RING == n % RING], default=0)


GATES_PAUSE = (1, 8)
OUT_MOST = 2

LN1, LN2, MIXPRE0, MIXPOST0, FFNPRE0, FFNPOST0, MIXPRE1, MIXPOST1, FFNPRE1, FFNPOST1 = range(10)
S_LN0 = 10
POST = (MIXPOST0, FFNPOST0, MIXPOST1, FFNPOST1)
PRE = (FFNPRE0, MIXPRE1, FFNPRE1)
X_LN0, X_O1, X_MIXED, X_LN1, X_POOL, X_FFN0, X_KV, X_Q, X_O2, X_FFN1 = range(10)

SWA_ORDER = [0, 4, 1, 5, 2, 6, 3, 7]
ORDER_2 = [0, 4, 1, 5, 2, 6, 3, 7, 8, 12, 9, 13, 10, 14, 11, 15]

PARAM_WIDTHS = [
    ("ln0_g", DC), ("ln0_b", DC), ("b_in", 34), ("b_out", DC), ("ln1_g", DC), ("ln1_b", DC),
    ("b_ff1", F1 // P), ("b_ff2", DC), ("ln2_g", DC), ("ln2_b", DC),
    ("mix_pre0", DC), ("mix_pre1", DC), ("mix_post0", DC), ("mix_post1", DC), ("pool_scale", DC),
    ("kv_g", DC), ("ffn_pre0", DC), ("ffn_pre1", DC), ("ffn_post0", DC), ("ffn_post1", DC),
    ("conv0", 16 * PAIRS2), ("conv1", 16 * PAIRS2), ("sink1", HEADS_SWA), ("sink2", HEADS_2),
]
CONST_WIDTHS = [
    ("na_mask", GRID_W), ("swa_mask", P + T), ("mask2", P + T), ("cos1", T), ("sin1", T),
    ("perm1", P), ("perm2", P), ("inv_freq2", 1), ("sign2", 1),
]


def offsets(widths):
    at, out = 0, {}
    for name, w in widths:
        out[name] = at
        at += w
    return out, at


PAR, N_PAR = offsets(PARAM_WIDTHS)
CON, N_CON = offsets(CONST_WIDTHS)

TWO_PI_PARTS = (6.25, 0.03125, 0.001934051513671875, 1.2556659146e-6)
ROUND_MAGIC = 12582912.0
PI_BELOW = 3.1415925


class Chain:

    def __init__(self, eng, sem):
        self.eng, self.sem, self.n, self.offset = eng, sem, 0, 0

    def link(self, ins):
        ins.then_inc(self.sem, 1)
        self.n += 1
        self.eng.wait_ge(self.sem, self.n + self.offset)

    def enter(self, i, steps):
        self.start, self.steps, self.offset = self.n, steps, i * steps

    def leave(self, rounds):
        assert self.n - self.start == self.steps, (self.n - self.start, self.steps)
        self.n, self.offset = self.start + rounds * self.steps, 0


class Straight:

    def unit(self, n):
        return n

    def landed(self, n):
        return 16 * (n // RING + 1)

    def up(self, q):
        return q

    def pair(self, j):
        return j


class Looped:

    def __init__(self, i, ups, pairs):
        self.i, self.ups, self.pairs = i, ups, pairs

    def unit(self, n):
        return n + 6 * self.i

    def landed(self, n):
        return 16 * (n // RING + 1) + 32 * self.i

    def up(self, q):
        return q + self.ups * self.i

    def pair(self, j):
        return j + self.pairs * self.i


STRAIGHT = Straight()
GLU_ROUNDS = (PAIRS2 - 5) // 2


def build(nc, x, w_stream, params, consts, bands, rpb, positions, out):
    ctx = ExitStack()
    with ctx:
        def sb(name, shape, dt=F32):
            return ctx.enter_context(nc.sbuf_tensor(name, shape, dt))

        def sem(name):
            return ctx.enter_context(nc.semaphore(name))

        w32 = [sb(f"w32_{s}", [P, UNIT]) for s in range(RING)]
        w_hi = [sb(f"w_hi{s}", [P, UNIT], F32R) for s in range(RING)]
        w_lo = [sb(f"w_lo{s}", [P, UNIT], F32R) for s in range(RING)]
        x_hi = [sb(f"x_hi{s}", [P, DC, T], F32R) for s in range(2)]
        x_lo = [sb(f"x_lo{s}", [P, DC, T], F32R) for s in range(2)]
        mid_hi = [sb(f"mid_hi{s}", [P, 2, T], F32R) for s in range(3)]
        mid_lo = [sb(f"mid_lo{s}", [P, 2, T], F32R) for s in range(3)]
        par = sb("par", [P, N_PAR])
        con = sb("con", [P, N_CON])
        ident = sb("ident", [P, P])
        inv_d = sb("inv_d", [P, 1])
        neg_half = sb("neg_half", [P, TT])
        half_gate_bias = sb("half_gate_bias", [P, 2 * DC])
        neg_sink1 = sb("neg_sink1", [P, HEADS_SWA])
        neg_sink2 = sb("neg_sink2", [P, HEADS_2])
        cos2 = sb("cos2", [P, T])
        sin2 = sb("sin2", [P, T])
        res = sb("res", [P, DC, T])
        proj = sb("proj", [P, 18, T])
        raw = proj[:, 0:DC, :]
        sq = proj[:, DC:2 * DC, :]
        rows = [sb(f"rows{s}", [P, 2 * T]) for s in range(2)]
        stat = sb("stat", [P, 11, 8])
        v_tok = sb("v_tok", [P, TT, HEADS_NA * HD])
        v_tok_swa = sb("v_tok_swa", [P, TT, P])
        BIAS_ROWS = GRID_ROWS + 2
        BIAS_W = BIAS_ROWS * GRID_W
        REGION = max(HEADS_NA * BIAS_W, 3104)
        region = sb("region", [P, REGION])
        bias_na = region[:, 0:HEADS_NA * BIAS_W].rearrange("p (h k) -> p h k", h=HEADS_NA)
        gates = sb("gates", [P, 2 * DC, T])
        scores = [sb(f"scores{s}", [P, 2 * T]) for s in range(2)]
        probs = [sb(f"probs{s}", [P, 2 * T]) for s in range(3)]
        probs_t = [sb(f"probs_t{s}", [P, 2 * T]) for s in range(2)]
        small = sb("small", [P, 5, 2 * 32])
        glu_u = [region[:, k * 2 * (T + 2):(k + 1) * 2 * (T + 2)].rearrange("p (t n) -> p t n", t=2)
                 for k in range(2)]
        glu_c = [region[:, 1056 + k * 2 * T:1056 + (k + 1) * 2 * T].rearrange("p (t n) -> p t n", t=2)
                 for k in range(2)]
        glu_g = region[:, 2080:2080 + 2 * T].rearrange("p (t n) -> p t n", t=2)
        glu_m = region[:, 2592:2592 + 2 * T].rearrange("p (t n) -> p t n", t=2)
        relu_v = glu_m
        gflat = gates[:, :, :].rearrange("p c n -> p (c n)")
        band = gflat[:, 0:len(POOL_WINDOWS) * BAND_W]
        x_tok = gates[:, 0:8, :].rearrange("p (t c) n -> p t (c n)", t=TT)
        xn_tok = gates[:, 8:16, :].rearrange("p (t c) n -> p t (c n)", t=TT)
        h_tok = xn_tok
        out_tok = x_tok
        pos_i = probs[0][:, 0:T].bitcast(I32)
        tmp_rot = [gates[:, 12:14, :], gates[:, 14:16, :]]
        angle = [scores[0][:, 0:T], scores[0][:, T:2 * T], scores[1][:, 0:T], scores[1][:, T:2 * T]]
        v_tok2 = v_tok[:, :, 0:4 * HD]

        up = [ctx.enter_context(nc.psum_tensor(f"up{b}", [P, 2 * T], F32)) for b in range(RING)]
        aux = ctx.enter_context(nc.psum_tensor("aux", [P, 2 * T], F32))
        down = [ctx.enter_context(nc.psum_tensor(f"down{b}", [P, 2 * T], F32)) for b in range(4)]

        diff = [*up, aux]

        mean_bank = {LN1: down[0], LN2: up[0]}

        x_landed = [sem(f"x_landed{t}") for t in range(TT)]
        par_landed = sem("par_landed")
        con_landed = sem("con_landed")
        pos_landed = sem("pos_landed")
        bias_landed = sem("bias_landed")
        w_landed = [sem(f"w_landed{s}") for s in range(RING)]
        w_hi_ready = sem("w_hi_ready")
        w_lo_ready = sem("w_lo_ready")
        unit_done = sem("unit_done")
        up_read = sem("up_read")
        x_hi_ready = sem("x_hi_ready")
        x_ready = sem("x_ready")
        const_ready = sem("const_ready")
        ident_zero = sem("ident_zero")
        small_ready = sem("small_ready")
        ln0_var = sem("ln0_var")
        ln0_rstd = sem("ln0_rstd")
        ln0_shift = sem("ln0_shift")
        xn_ready = sem("xn_ready")
        ln0_turned = sem("ln0_turned")
        ln0_h = sem("ln0_h")
        angle_ready = sem("angle_ready")
        trig_ready = sem("trig_ready")
        bias_ready = sem("bias_ready")
        dve_chain = sem("dve_chain")
        act_chain = sem("act_chain")
        pool_chain = sem("pool_chain")
        raw_ready = sem("raw_ready")
        sq_ready = sem("sq_ready")
        sum_ready = sem("sum_ready")
        mean_ready = sem("mean_ready")
        stat_done = sem("stat_done")
        var_ready = sem("var_ready")
        rstd_ready = sem("rstd_ready")
        rows_done = sem("rows_done")
        rows_ready = sem("rows_ready")
        scaled_ready = sem("scaled_ready")
        pool_added = sem("pool_added")
        dve_added = sem("dve_added")
        mean_done = sem("mean_done")
        mean_col = sem("mean_col")
        mean_off = sem("mean_off")
        normed_ready = sem("normed_ready")
        res_act_ready = sem("res_act_ready")
        res_pool_ready = sem("res_pool_ready")
        band_landed = sem("band_landed")
        res_turned = sem("res_turned")
        h_act_ready = sem("h_act_ready")
        h_dve_ready = sem("h_dve_ready")
        res_b_ready = sem("res_b_ready")
        rot_done = sem("rot_done")
        rot_read = sem("rot_read")
        rot_ready = sem("rot_ready")
        v_turned = sem("v_turned")
        v_ready = sem("v_ready")
        s_done = sem("s_done")
        s_ready = sem("s_ready")
        negmax_ready = sem("negmax_ready")
        p_ready = sem("p_ready")
        rden_ready = sem("rden_ready")
        pn_ready = sem("pn_ready")
        pt_done = sem("pt_done")
        pt_ready = sem("pt_ready")
        o_done = sem("o_done")
        mixed_ready = sem("mixed_ready")
        down_done = sem("down_done")
        glu_ready = sem("glu_ready")
        conv_first = sem("conv_first")
        conv_ready = sem("conv_ready")
        gelu_ready = sem("gelu_ready")
        mid_f32 = sem("mid_f32")
        mid_hi_ready = sem("mid_hi_ready")
        mid_ready = sem("mid_ready")
        diff_done = sem("diff_done")
        out_turned = sem("out_turned")
        out_act_ready = sem("out_act_ready")
        out_dve_ready = sem("out_dve_ready")
        out_stored = sem("out_stored")

        block = ctx.enter_context(nc.Block())

        def pcol(name, c, n=1):
            return par[:, PAR[name] + c:PAR[name] + c + n]

        def pdyn(name, c, n=1):
            return par[:, bass.ds(PAR[name] + c, n)]

        def ccol(name, c=0, n=1):
            return con[:, CON[name] + c:CON[name] + c + n]

        def shifted(handle, width, offset):
            return bass.AP(handle[:, :].tensor, offset + P, [[width, P], [-P, 2], [1, T]])

        def pair_view(ap):
            return ap.rearrange("p (t n) -> p t n", t=2)

        def twice(ap):
            return ap.unsqueeze(1).to_broadcast([P, 2, T])

        hi_count, at_ = {}, 0
        for f in range(10):
            hi_count[f] = at_
            at_ += 4 if f == X_MIXED else DC

        def hi_ready(fill, c):
            return hi_count[fill] + (c // 2 if fill == X_MIXED else c) + 1

        def rows_before(k):
            return k - (k > MIXPRE0)

        def wait_rows_used(e, k):
            if k in (LN1, LN2):
                e.wait_ge(normed_ready, DC * (k + 1))
            elif k == MIXPRE0:
                e.wait_ge(var_ready, k + 1)
            elif k in POST:
                e.wait_ge(scaled_ready, 4 * (POST.index(k) + 1))
            else:
                e.wait_ge(rows_ready, PRE.index(k) + 1)

        def wait_added(e, index, gr):
            if gr in (0, 3):
                e.wait_ge(dve_added, 2 * index + gr // 3 + 1)
            else:
                e.wait_ge(pool_added, 2 * index + gr)

        def add_group(engine, e, chain, total, values, step, wait_group):
            if step == 1:
                wait_group(0)
            wait_group(step)
            first = values[:, 0:2, :] if step == 1 else total
            chain.link(engine.tensor_tensor(total, first, values[:, 2 * step:2 * step + 2, :], ALU.add))
            if step < 3:
                return None
            return engine.tensor_tensor(total[:, 0, :], total[:, 0, :], total[:, 1, :], ALU.add)

        def add_squares(engine, e, chain, k, step):
            ins = add_group(engine, e, chain, sq[:, 0:2, :], sq, step, lambda gr: e.wait_ge(sq_ready, 4 * k + gr + 1))
            if ins is not None:
                ins.then_inc(sum_ready, 1)

        def mean_total(k):
            return rows[(k + 1) % 2][:, :].rearrange("p (t n) -> p t n", t=2)

        DOWN_BASE = {U_FF: 0, U_POOL: 3, U_GLU0: 6, U_GLU1: 9}

        @block.sync
        def _(sp):
            for t in range(TT):
                sp.dma_start(x_tok[:, t, :], x[t * P:(t + 1) * P, :]).then_inc(x_landed[t], 16)
            for n in range(RING):
                sp.dma_start(w32[n][:, :], w_stream[n]).then_inc(w_landed[n], 16)
                if n == 0:
                    sp.dma_start(par[:, :], params).then_inc(par_landed, 16)
            sp.dma_start(con[:, :], consts).then_inc(con_landed, 16)
            sp.dma_start(pos_i[:, :], positions.partition_broadcast(P)).then_inc(pos_landed, 16)
            for rr in range(2):
                first = GRID_ROWS - 3 - rr
                sp.dma_start(bias_na[rr * GRID_W:(rr + 1) * GRID_W, :, :],
                             rpb[:, :, first * GRID_W:(first + BIAS_ROWS) * GRID_W]).then_inc(bias_landed, 16)
            rounds = N_UNITS // RING - 1
            with sp.Fori(0, rounds) as i:
                for s in range(RING):
                    sp.wait_ge(w_lo_ready, s + 1 + RING * i)
                    sp.dma_start(w32[s][:, :], w_stream[bass.ds(RING + s + RING * i, 1), :, :].rearrange("a p n -> p (a n)"))\
                        .then_inc(w_landed[s], 16)
            for n in range(RING * (rounds + 1), N_UNITS):
                sp.wait_ge(w_lo_ready, n - RING + 1)
                sp.dma_start(w32[n % RING][:, :], w_stream[n]).then_inc(w_landed[n % RING], 16)
            for half, ready in enumerate((out_act_ready, out_dve_ready)):
                for t in range(TT):
                    sp.wait_ge(ready, t + 1)
                    sp.dma_start(out[t * P:(t + 1) * P, half * 2 * T:(half + 1) * 2 * T],
                                 out_tok[:, t, half * 2 * T:(half + 1) * 2 * T]).then_inc(out_stored, 16)
            sp.wait_ge(out_stored, 16 * 2 * TT)

        @block.gpsimd
        def _(pool):
            chain = Chain(pool, pool_chain)
            g = nc.gpsimd
            g.memset(inv_d[:, :], 1.0 / D)
            g.memset(neg_half[:, :], -0.5)
            g.memset(ident[:, :], 0.0).then_inc(ident_zero, 1)
            pool.wait_ge(ident_zero, 1)
            g.affine_select(out=ident[:, :], in_=ident[:, :], compare_op=ALU.not_equal, fill=1.0, base=0,
                            pattern=[[-1, P]], channel_multiplier=1).then_inc(const_ready, 1)
            pool.wait_ge(ln0_var, 1)
            pool.wait_ge(const_ready, 1)
            g.tensor_tensor(stat[:, S_LN0, 2:4], stat[:, S_LN0, 0:2], neg_half[:, :], ALU.pow).then_inc(ln0_rstd, 1)
            pool.wait_ge(con_landed, 16)
            pool.wait_ge(bias_landed, 16 * 2)
            rows_all = region[:, 0:HEADS_NA * BIAS_W].rearrange("p (r k) -> p r k", k=GRID_W)
            g.tensor_tensor(rows_all, rows_all,
                            ccol("na_mask", 0, GRID_W).unsqueeze(1).to_broadcast([P, HEADS_NA * BIAS_ROWS, GRID_W]),
                            ALU.add).then_inc(bias_ready, 1)

            def residual_plus_bias(bias, fill):
                for c in range(DC):
                    pool.wait_ge(x_ready, DC * fill + c + 1)
                    ins = g.tensor_scalar(res[:, c, :], res[:, c, :], ALPHA, pcol(bias, c), ALU.mult, ALU.add)
                    if c % 2:
                        ins.then_inc(res_b_ready, 1)

            def split_low(n):
                pool.wait_ge(w_lo_ready, n)
                pool.wait_ge(w_hi_ready, n + 1)
                g.tensor_tensor(w_lo[n % RING][:, :], w32[n % RING][:, :], w_hi[n % RING][:, :].bitcast(F32), ALU.subtract)\
                    .then_inc(w_lo_ready, 1)

            def inverse_root(k, ready):
                pool.wait_ge(ready, k + 1)
                g.tensor_tensor(stat[:, k, 2:4], stat[:, k, 0:2], neg_half[:, :], ALU.pow).then_inc(rstd_ready, 1)

            def add_residual(index):
                for gr in (1, 2):
                    pool.wait_ge(scaled_ready, 4 * index + gr + 1)
                    g.tensor_tensor(res[:, 2 * gr:2 * gr + 2, :], res[:, 2 * gr:2 * gr + 2, :],
                                    raw[:, 2 * gr:2 * gr + 2, :], ALU.add).then_inc(pool_added, 1)

            def add_values(k, wait_group):
                for step in range(1, 4):
                    ins = add_group(g, pool, chain, mean_total(k), raw, step, wait_group)
                ins.then_inc(mean_ready, 1)

            def square_sum(k):
                for step in range(1, 4):
                    add_squares(g, pool, chain, k, step)

            def normalise(h, spans):
                pool.wait_ge(rden_ready, h + 1)
                p = probs[h % 3]
                for t, (a, b) in enumerate(spans):
                    ins = g.tensor_scalar(p[:, a:b], p[:, a:b], small[:, 4, 2 * h + t:2 * h + t + 1], 1.0,
                                          ALU.mult, ALU.mult)
                ins.then_inc(pn_ready, 1)

            pool.wait_ge(par_landed, 16)
            residual_plus_bias("b_out", X_LN0)
            for h in range(16):
                normalise(h, [(0, T), (T, 2 * T)])
            add_values(LN1, lambda gr: pool.wait_ge(up_read, UP_INDEX[U_WOUT + gr] + 1))
            inverse_root(LN1, var_ready)
            for c in range(DC):
                pool.wait_ge(normed_ready, c + 1)
                chain.link(g.tensor_scalar(res[:, c, :], raw[:, c, :], pcol("ln1_b", c), ALPHA, ALU.add, ALU.mult))
                ins = g.tensor_scalar(res[:, c, :], res[:, c, :], 1.0, pcol("b_ff2", c), ALU.mult, ALU.add)
                if c % 2:
                    ins.then_inc(res_b_ready, 1)
            add_values(LN2, lambda gr: pool.wait_ge(raw_ready, gr + 1))
            inverse_root(LN2, var_ready)
            for c in range(4, DC):
                pool.wait_ge(normed_ready, DC + c + 1)
                g.tensor_scalar(res[:, c, :], raw[:, c, :], 1.0, pcol("ln2_b", c), ALU.mult, ALU.add)\
                    .then_inc(res_pool_ready, 1)
            inverse_root(MIXPRE0, var_ready)
            split_low(U_POOL - 1 + RING)
            inverse_root(MIXPOST0, var_ready)
            add_residual(0)
            square_sum(FFNPRE0)
            inverse_root(FFNPRE0, var_ready)

            def glu_products(rounds, base):
                def product(at, j, j0):
                    pool.wait_ge(gelu_ready, at.pair(j + 1))
                    pool.wait_ge(conv_ready, at.pair(j + 1))
                    if j > j0:
                        pool.wait_ge(mid_ready, PAIRS1 + at.pair(j))
                    g.tensor_tensor(glu_m, glu_g, glu_c[1], ALU.mult).then_inc(mid_f32, 1)
                product(STRAIGHT, rounds, rounds)
                with pool.Fori(0, (PAIRS2 - 3) // 2) as i:
                    at = Looped(i, 4, 2)
                    product(at, rounds + 1, rounds)
                    product(at, rounds + 2, rounds)
                product(STRAIGHT, rounds + PAIRS2 - 2, rounds)
                split_low(base + 3 * PAIRS2 - 1)
                product(STRAIGHT, rounds + PAIRS2 - 1, rounds)
                if base + 3 * PAIRS2 < N_UNITS:
                    split_low(base + 3 * PAIRS2)

            glu_products(0, U_GLU0)
            inverse_root(FFNPOST0, var_ready)
            add_residual(1)
            square_sum(MIXPRE1)
            inverse_root(MIXPRE1, var_ready)
            for h in range(16, 32):
                normalise(h, [(0, P), (P, P + T)])
            inverse_root(MIXPOST1, var_ready)
            add_residual(2)
            square_sum(FFNPRE1)
            inverse_root(FFNPRE1, var_ready)
            glu_products(PAIRS2, U_GLU1)
            inverse_root(FFNPOST1, var_ready)
            add_residual(3)

        @block.scalar
        def _(act):
            chain = Chain(act, act_chain)
            a = nc.scalar

            def split(at, n):
                s = n % RING
                if n >= RING:
                    act.wait_ge(unit_done, at.unit(n - RING + 1))
                act.wait_ge(w_landed[s], at.landed(n))
                a.activation(w_hi[s][:, :], w32[s][:, :], ACT.Copy).then_inc(w_hi_ready, 1)

            def square(k, gr, src, ready=None, value=0):
                if ready is not None:
                    act.wait_ge(ready, value)
                if k:
                    act.wait_ge(stat_done, k)
                a.activation(sq[:, 2 * gr:2 * gr + 2, :], src, ACT.Square).then_inc(sq_ready, 1)

            def next_split(at, n):
                if n + RING < N_UNITS:
                    split(at, n + RING)

            act.wait_ge(ln0_shift, 1)
            a.activation(xn_tok[:, 0, :], x_tok[:, 0, :], ACT.Identity, bias=stat[:, S_LN0, 4:5],
                         scale=stat[:, S_LN0, 2:3]).then_inc(xn_ready, 1)
            split(STRAIGHT, 0)
            act.wait_ge(par_landed, 16)
            for c in range(DC):
                if c % 2 == 0:
                    act.wait_ge(ln0_turned, c // 2 + 1)
                a.activation(res[:, c, :], down[c // 2][:, (c % 2) * T:(c % 2 + 1) * T], ACT.Identity,
                             bias=pcol("ln0_b", c), scale=pcol("ln0_g", c)).then_inc(ln0_h, 1)
            split(STRAIGHT, 1)
            split(STRAIGHT, 2)

            def rotary_tables():
                act.wait_ge(angle_ready, 1)
                a.activation(sin2[:, :], angle[0], ACT.Sin).then_inc(trig_ready, 1)
                act.wait_ge(angle_ready, 2)
                a.activation(cos2[:, :], angle[1], ACT.Sin).then_inc(trig_ready, 1)

            for n in range(U_QKV, U_GATE):
                if n == U_QKV + 2:
                    rotary_tables()
                act.wait_ge(unit_done, n + 1)
                for t in range(2):
                    ins = a.activation(proj[:, 2 * n + t, :], up[n % RING][:, t * T:(t + 1) * T], ACT.Identity,
                                       bias=pcol("b_in", 2 * n + t))
                ins.then_inc(up_read, 1)
                next_split(STRAIGHT, n)

            def exps(h, spans, sink):
                act.wait_ge(negmax_ready, h + 1)
                if h >= 3:
                    act.wait_ge(pt_done, h - 2)
                for t, (lo, hi) in enumerate(spans):
                    ins = a.activation(probs[h % 3][:, lo:hi], scores[h % 2][:, lo:hi], ACT.Exp,
                                       bias=small[:, 0, 2 * h + t:2 * h + t + 1],
                                       accum_out=small[:, 1, 2 * h + t:2 * h + t + 1])
                if sink is not None:
                    ins = a.activation(small[:, 2, 2 * h:2 * h + 2], small[:, 0, 2 * h:2 * h + 2], ACT.Exp, bias=sink)
                ins.then_inc(p_ready, 1)

            def probs_out(h, width):
                act.wait_ge(pt_done, h + 1)
                if h >= 2:
                    act.wait_ge(o_done, h - 1)
                a.activation(probs_t[h % 2][:, 0:width], down[2][:, 0:width], ACT.Copy).then_inc(pt_ready, 1)

            def attention_out(h, fill, chunk):
                act.wait_ge(o_done, h + 1)
                bank = (down[3], aux)[chunk % 2]
                a.activation(x_hi[fill % 2][:, chunk, :], bank[:, 0:T], ACT.Copy).then_inc(x_hi_ready, 1)

            def sink1(h):
                return None if h < 8 else pcol("sink1", h - 8)

            spans1 = [(0, T), (T, 2 * T)]
            exps(0, spans1, None)
            exps(1, spans1, None)
            for h in range(16):
                if h == 0:
                    act.wait_ge(small_ready, 1)
                if h % 2 == 1:
                    n = U_GATE + h // 2
                    act.wait_ge(unit_done, n + 1)
                    for t in range(2):
                        c = 2 * (n - U_GATE) + t
                        ins = a.activation(gates[:, c, :], up[n % RING][:, t * T:(t + 1) * T], ACT.Tanh,
                                           bias=half_gate_bias[:, c:c + 1], scale=0.5)
                    ins.then_inc(up_read, 1)
                probs_out(h, 2 * T)
                if h + 2 < 16:
                    exps(h + 2, spans1, sink1(h + 2))
                if h % 2 == 1:
                    next_split(STRAIGHT, U_GATE + h // 2)
                if h % 2 == 0 and h >= 2:
                    attention_out(h - 1, X_O1, h // 2 - 1)
            attention_out(15, X_O1, 7)

            for half in range(2):
                next_split(STRAIGHT, U_BRANCH + 2 * half)
                for gr in range(2 * half, 2 * half + 2):
                    act.wait_ge(mixed_ready, gr + 1)
                    a.activation(x_hi[X_MIXED % 2][:, 2 * gr:2 * gr + 2, :], raw[:, 2 * gr:2 * gr + 2, :], ACT.Copy,
                                 scale=0.5).then_inc(x_hi_ready, 1)
                next_split(STRAIGHT, U_BRANCH + 2 * half + 1)

            def squares_of_sum(k, index):
                for gr in range(4):
                    square(k, gr, raw[:, 2 * gr:2 * gr + 2, :], raw_ready, 4 * index + gr + 1)

            def squares_of_units(k, units):
                for gr in range(4):
                    if units == U_WO and gr < 3:
                        next_split(STRAIGHT, units + gr)
                    square(k, gr, raw[:, 2 * gr:2 * gr + 2, :], up_read, UP_INDEX[units + gr] + 1)
                    if units != U_WO and gr < 3:
                        next_split(STRAIGHT, units + gr)

            act.wait_ge(mixed_ready, 4)
            act.dma_start(band, bands).then_inc(band_landed, 16)
            squares_of_units(LN1, U_WOUT)
            for c in range(DC):
                act.wait_ge(normed_ready, c + 1)
                a.activation(x_hi[X_LN1 % 2][:, c, :], raw[:, c, :], ACT.Identity, bias=pcol("ln1_b", c))\
                    .then_inc(x_hi_ready, 1)
            next_split(STRAIGHT, U_WOUT + 3)

            def relu_square(at, n, j):
                s = n % RING
                act.wait_ge(unit_done, at.unit(n + 1))
                if j:
                    act.wait_ge(mid_ready, at.pair(j))
                for t in range(2):
                    ins = a.activation(relu_v[:, t, :], up[s][:, t * T:(t + 1) * T], ACT.Relu,
                                       bias=pdyn("b_ff1", 2 * at.pair(j) + t))
                ins.then_inc(up_read, 1)
                act.wait_ge(up_read, at.up(UP_INDEX[n] + 1))
                a.activation(mid_hi[j % 3][:, :, :], relu_v, ACT.Square).then_inc(mid_hi_ready, 1)

            def ff_units(at, j):
                relu_square(at, U_FF + 2 * j - 1, j)
                next_split(at, U_FF + 2 * j - 1)
                next_split(at, U_FF + 2 * j)

            relu_square(STRAIGHT, U_FF, 0)
            next_split(STRAIGHT, U_FF)
            for j in range(1, 4):
                ff_units(STRAIGHT, j)
            with act.Fori(0, (PAIRS1 - 4) // 3) as i:
                at = Looped(i, 3, 3)
                for j in range(4, 7):
                    ff_units(at, j)
            squares_of_sum(LN2, 0)
            act.wait_ge(stat_done, MIXPRE0)
            for c in range(DC):
                act.wait_ge(normed_ready, DC + c + 1)
                ins = a.activation(sq[:, c, :], raw[:, c, :], ACT.Square, bias=pcol("ln2_b", c))
                if c % 2:
                    ins.then_inc(sq_ready, 1)
                if c < 4:
                    a.activation(res[:, c, :], raw[:, c, :], ACT.Identity, bias=pcol("ln2_b", c))\
                        .then_inc(res_act_ready, 1)
            next_split(STRAIGHT, U_FF + 2 * PAIRS1 - 1)

            act.wait_ge(rstd_ready, MIXPRE0 + 1)
            for half in range(2):
                act.wait_ge(res_turned, 2 * half + 1)
                a.activation(h_tok[:, 0, half * 2 * T:(half + 1) * 2 * T], down[half][:, :], ACT.Copy,
                             scale=stat[:, MIXPRE0, 2:3]).then_inc(h_act_ready, 1)
            for c in range(DC):
                if c % 2 == 0:
                    act.wait_ge(diff_done, c // 2 + 1)
                a.activation(x_hi[X_POOL % 2][:, c, :], diff[c // 2][:, (c % 2) * T:(c % 2 + 1) * T], ACT.Copy,
                             scale=pcol("mix_pre0", c)).then_inc(x_hi_ready, 1)
            squares_of_sum(MIXPOST0, 1)
            next_split(STRAIGHT, U_POOL)

            def fill(k, index, fills):
                for gr in range(4):
                    wait_added(act, index, gr)
                    name, which = fills[0]
                    for c in (2 * gr, 2 * gr + 1):
                        a.activation(x_hi[which % 2][:, c, :], res[:, c, :], ACT.Copy, scale=pcol(name, c))\
                            .then_inc(x_hi_ready, 1)
                    square(k, gr, res[:, 2 * gr:2 * gr + 2, :])
                for name, which in fills[1:]:
                    for c in range(DC):
                        a.activation(x_hi[which % 2][:, c, :], res[:, c, :], ACT.Copy, scale=pcol(name, c))\
                            .then_inc(x_hi_ready, 1)

            def glu_pair(at, base, layer, j):
                first = PAIRS2 * layer
                units = (base + 3 * j - 1, base + 3 * j) if j else (base, base + 1)
                for kind in range(2):
                    act.wait_ge(up_read, at.up(UP_INDEX[units[kind]] + 1))
                    if layer or j:
                        act.wait_ge(mid_f32, at.pair(first + j))
                    for t in range(2):
                        col = 16 * at.pair(j) + 8 * kind + 4 * t
                        ins = a.activation(glu_c[kind][:, t, :], glu_u[kind][:, t, 2:T + 2], ACT.Identity,
                                           bias=pdyn(f"conv{layer}", col + 3), scale=pdyn(f"conv{layer}", col + 2))
                    ins.then_inc(conv_first, 1)
                    if kind == 0 and j:
                        next_split(at, units[0])
                act.wait_ge(glu_ready, at.pair(first + j + 1))
                a.activation(glu_g, glu_c[0], ACT.Gelu_apprx_tanh).then_inc(gelu_ready, 1)
                if j < PAIRS2 - 1:
                    next_split(at, units[1])
                act.wait_ge(mid_f32, at.pair(first + j + 1))
                a.activation(mid_hi[j % 2][:, :, :], glu_m, ACT.Copy).then_inc(mid_hi_ready, 1)
                if j == PAIRS2 - 1:
                    next_split(at, units[1])
                if j:
                    next_split(at, base + 3 * j + 1)

            def glu(base, layer):
                next_split(STRAIGHT, base)
                glu_pair(STRAIGHT, base, layer, 0)
                glu_pair(STRAIGHT, base, layer, 1)
                glu_pair(STRAIGHT, base, layer, 2)
                with act.Fori(0, GLU_ROUNDS) as i:
                    at = Looped(i, 4, 2)
                    glu_pair(at, base, layer, 3)
                    glu_pair(at, base, layer, 4)
                for j in range(3 + 2 * GLU_ROUNDS, PAIRS2):
                    glu_pair(STRAIGHT, base, layer, j)

            fill(FFNPRE0, 0, [("ffn_pre0", X_FFN0)])
            glu(U_GLU0, 0)
            squares_of_sum(FFNPOST0, 2)
            next_split(STRAIGHT, U_GLU0 + 3 * PAIRS2 - 1)
            fill(MIXPRE1, 1, [("kv_g", X_KV), ("mix_pre1", X_Q)])

            spans2 = [(0, P), (P, P + T)]

            def sink2(h):
                return pcol("sink2", h)

            next_split(STRAIGHT, U_KV)
            next_split(STRAIGHT, U_KV + 1)
            next_split(STRAIGHT, U_Q)
            exps(16, spans2, sink2(0))
            exps(17, spans2, sink2(1))
            for h in range(16):
                if h + 2 < 16:
                    exps(16 + h + 2, spans2, sink2(h + 2))
                probs_out(16 + h, P + T)
                if h == 0:
                    next_split(STRAIGHT, U_Q + 1)
                if h in (2, 6):
                    next_split(STRAIGHT, U_Q + 2 + h // 4)
                if h % 2 == 0 and h >= 2:
                    attention_out(16 + h - 1, X_O2, h // 2 - 1)
            attention_out(31, X_O2, 7)
            squares_of_units(MIXPOST1, U_WO)
            next_split(STRAIGHT, U_WO + 3)
            fill(FFNPRE1, 2, [("ffn_pre1", X_FFN1)])
            glu(U_GLU1, 1)
            squares_of_sum(FFNPOST1, 3)
            for t in range(TT):
                act.wait_ge(out_turned, t + 1)
                a.activation(out_tok[:, t, 0:2 * T], down[2 * t][:, :], ACT.Copy).then_inc(out_act_ready, 1)

        @block.tensor
        def _(pe):
            m = nc.tensor.matmul

            def product(out_ap, w_cols, slot, xh, xl, first, last):
                m(out_ap, w_hi[slot][:, w_cols:w_cols + P], xl, start=first, stop=False, skip_group_check=True)
                m(out_ap, w_hi[slot][:, w_cols:w_cols + P], xh, start=False, stop=False, skip_group_check=True)
                return m(out_ap, w_lo[slot][:, w_cols:w_cols + P], xh, start=False, stop=last, skip_group_check=True)

            def tile(at, n, t, fill, chunks_from=None):
                s = n % RING
                if t == 0:
                    pe.wait_ge(w_lo_ready, at.unit(n + 1))
                    if reads_before(n):
                        pe.wait_ge(up_read, at.up(reads_before(n)))
                for c in range(DC):
                    if chunks_from is not None and t == 0:
                        pe.wait_ge(x_ready, chunks_from + c + 1)
                    ins = product(up[s][:, t * T:(t + 1) * T], c * UC + t * P, s, x_hi[fill % 2][:, c, :],
                                  x_lo[fill % 2][:, c, :], c == 0, c == DC - 1)
                if t == 1:
                    ins.then_inc(unit_done, 1)

            def first_unit(n, fill):
                s = n % RING
                pe.wait_ge(w_lo_ready, n + 1)
                if reads_before(n):
                    pe.wait_ge(up_read, reads_before(n))
                for c in range(DC):
                    if c % 2 == 0 or fill != X_MIXED:
                        pe.wait_ge(x_hi_ready, hi_ready(fill, c))
                    for w in (w_hi[s], w_lo[s]):
                        for t in range(2):
                            m(up[s][:, t * T:(t + 1) * T], w[:, c * UC + t * P:c * UC + (t + 1) * P],
                              x_hi[fill % 2][:, c, :], start=(c == 0 and t == 0 and w is w_hi[s]), stop=False,
                              skip_group_check=True)
                for c in range(DC):
                    pe.wait_ge(x_ready, DC * fill + c + 1)
                    for t in range(2):
                        ins = m(up[s][:, t * T:(t + 1) * T], w_hi[s][:, c * UC + t * P:c * UC + (t + 1) * P],
                                x_lo[fill % 2][:, c, :], start=False, stop=(c == DC - 1), skip_group_check=True)
                ins.then_inc(unit_done, 1)

            def unit(at, n, fill, chunks_from=None):
                tile(at, n, 0, fill, chunks_from)
                tile(at, n, 1, fill)

            def sum_unit(at, n, j, slots, first, last):
                s = n % RING
                pe.wait_ge(w_lo_ready, at.unit(n + 1))
                for o in range(DC):
                    for c in range(2):
                        ins = product(down[o // 2][:, (o % 2) * T:(o % 2 + 1) * T], c * D + o * P, s,
                                      mid_hi[j % slots][:, c, :], mid_lo[j % slots][:, c, :],
                                      first and c == 0 and o % 2 == 0, last and c == 1)
                    if last and o % 2 == 1 and o < DC - 1:
                        ins.then_inc(down_done, 1)
                ins.then_inc(unit_done, 1)

            def statistics(k, with_mean):
                if k:
                    wait_rows_used(pe, k - 1)
                pe.wait_ge(sum_ready, k + 1)
                for t in range(TT):
                    ins = m(aux[:, t:t + 1], sq[:, 0, t * P:(t + 1) * P], inv_d[:, :], start=(t == 0), stop=True,
                            skip_group_check=True)
                if with_mean:
                    pe.wait_ge(mean_ready, k + 1)
                    for t in range(TT):
                        ins = m(aux[:, 2 + t:3 + t], mean_total(k)[:, 0, t * P:(t + 1) * P], inv_d[:, :], start=False,
                                stop=True, skip_group_check=True)
                ins.then_inc(stat_done, 1)

            def spread_column(out_ap, k, col):
                for t in range(TT):
                    ins = m(out_ap[:, t * P:(t + 1) * P], stat[:, k, col + t:col + t + 1].to_broadcast([P, P]), ident[:, :],
                            start=True, stop=True, skip_group_check=True)
                return ins

            def spread(k, with_mean):
                if with_mean:
                    pe.wait_ge(mean_col, k + 1)
                    spread_column(mean_bank[k], k, 6).then_inc(mean_done, 1)
                pe.wait_ge(rstd_ready, k + 1)
                spread_column(aux, k, 2).then_inc(rows_done, 1)

            pe.wait_ge(const_ready, 1)
            pe.wait_ge(xn_ready, 2)
            for c in range(DC):
                for t in range(TT):
                    ins = nc.tensor.transpose(down[c // 2][:, (c % 2) * T + t * P:(c % 2) * T + (t + 1) * P],
                                              xn_tok[:, t, c * P:(c + 1) * P], ident[:, :])
                if c % 2:
                    ins.then_inc(ln0_turned, 1)
            for n in range(U_QKV, U_GATE):
                if n == 0:
                    first_unit(n, X_LN0)
                else:
                    unit(STRAIGHT, n, X_LN0)

            def gate_tile(k):
                tile(STRAIGHT, U_GATE + k // 2, k % 2, X_LN0)

            gate_tile(0)
            pe.wait_ge(up_read, 6)
            pe.wait_ge(x_ready, DC)
            for tl in range(4):
                for kc in range(TT):
                    col = (tl % 2) * T + kc * P
                    ins = nc.tensor.transpose(down[2 + tl // 2][:, col:col + P], proj[:, 8 + tl, kc * P:(kc + 1) * P],
                                              ident[:, :])
                if tl % 2:
                    ins.then_inc(v_turned, 1)
            pe.wait_ge(con_landed, 16)
            for tl in range(4):
                if tl == 0:
                    pe.wait_ge(up_read, 8)
                ins = m(down[tl // 2][:, (tl % 2) * T:(tl % 2 + 1) * T], ccol("perm1", 0, P), proj[:, 12 + tl, :],
                        start=(tl % 2 == 0), stop=True, skip_group_check=True)
                if tl % 2:
                    ins.then_inc(rot_done, 1)
            pe.wait_ge(up_read, 9)
            m(aux[:, 0:T], ccol("perm1", 0, P), proj[:, 16, :], start=True, stop=True, skip_group_check=True)\
                .then_inc(rot_done, 1)
            for kc in range(TT):
                ins = nc.tensor.transpose(aux[:, T + kc * P:T + (kc + 1) * P], proj[:, 17, kc * P:(kc + 1) * P], ident[:, :])
            ins.then_inc(v_turned, 1)

            def score(h, q_tile, k_tile, half, plan):
                if h >= 2:
                    pe.wait_ge(s_ready, h - 1)
                rows_ = slice(half * HD, (half + 1) * HD)
                for k, (col, t, keys) in enumerate(plan):
                    ins = m(down[h % 2][:, col:col + keys], proj[rows_, q_tile, t * P:(t + 1) * P],
                            proj[rows_, k_tile, 0:keys], start=(k == 0), stop=True, skip_group_check=True)
                ins.then_inc(s_done, 1)

            def turn(h, plan):
                pe.wait_ge(pn_ready, h + 1)
                if h >= 1:
                    pe.wait_ge(pt_ready, h)
                for src, dst in plan:
                    ins = nc.tensor.transpose(down[2][:, dst:dst + P], probs[h % 3][:, src:src + P], ident[:, :])
                ins.then_inc(pt_done, 1)

            def attend(h, step, fill, half, v, plan):
                pe.wait_ge(pt_ready, h + 1)
                if half == 0 and step // 2 >= 2:
                    pe.wait_ge(x_ready, DC * fill + step // 2 - 1)
                bank = (down[3], aux)[(step // 2) % 2]
                for k, (kc, src, width, q0) in enumerate(plan):
                    ins = m(bank[half * HD:(half + 1) * HD, q0:q0 + width], v(kc), probs_t[h % 2][:, src:src + width],
                            start=(k == 0), stop=(k == len(plan) - 1), skip_group_check=True)
                ins.then_inc(o_done, 1)

            full = [(0, 0, T), (T, 1, T)]
            full_turn = [(t * T + kc * P, kc * T + t * P) for kc in range(TT) for t in range(TT)]
            full_attend = [(kc, kc * T, T, 0) for kc in range(TT)]

            def score1(h):
                if h == 0:
                    pe.wait_ge(rot_read, 2)
                if h == 8:
                    pe.wait_ge(rot_ready, 3)
                if h < 8:
                    score(h, h // 2, 4 + h // 2, h % 2, full)
                else:
                    score(h, 12 + (h - 8) // 2, 16, h % 2, full)

            def attend1(h):
                if h == 0:
                    pe.wait_ge(v_ready, 3)
                    pe.wait_ge(rot_read, 3)

                def v(kc):
                    if h < 8:
                        return v_tok[:, kc, h * HD:(h + 1) * HD]
                    return v_tok_swa[:, kc, (h % 2) * HD:(h % 2 + 1) * HD]
                attend(h, h, X_O1, h % 2, v, full_attend)

            score1(0)
            score1(1)
            gate_tile(1)
            for h in range(16):
                if h + 2 < 16:
                    score1(h + 2)
                if h not in GATES_PAUSE:
                    gate_tile(h + 2 - sum(h > pause for pause in GATES_PAUSE))
                if h == 0:
                    pe.wait_ge(v_ready, 2)
                turn(h, full_turn)
                if h:
                    attend1(h - 1)
            attend1(15)
            for q in range(4):
                n = U_BRANCH + q
                s = n % RING
                pe.wait_ge(w_lo_ready, n + 1)
                branch = q % 2
                pe.wait_ge(x_ready, DC * X_O1 + 4 * branch + 4)
                for o in range(4):
                    b = 2 * branch + o // 2
                    if q >= 2 and o % 2 == 0:
                        pe.wait_ge(mixed_ready, o // 2 + 1)
                    for c in range(4):
                        ins = product(down[b][:, (o % 2) * T:(o % 2 + 1) * T], c * 512 + o * P, s,
                                      x_hi[X_O1 % 2][:, 4 * branch + c, :], x_lo[X_O1 % 2][:, 4 * branch + c, :],
                                      c == 0 and o % 2 == 0, c == 3)
                ins.then_inc(unit_done, 1)
            for gr in range(4):
                if gr == 0:
                    first_unit(U_WOUT, X_MIXED)
                else:
                    unit(STRAIGHT, U_WOUT + gr, X_MIXED)
            statistics(LN1, True)
            spread(LN1, True)
            first_unit(U_FF, X_LN1)

            def ff_units(at, j):
                unit(at, U_FF + 2 * j - 1, X_LN1)
                pe.wait_ge(mid_ready, at.pair(j))
                sum_unit(at, U_FF + 2 * j, j - 1, 3, j == 1, False)

            for j in range(1, 4):
                ff_units(STRAIGHT, j)
            with pe.Fori(0, (PAIRS1 - 4) // 3) as i:
                at = Looped(i, 3, 3)
                for j in range(4, 7):
                    ff_units(at, j)
            pe.wait_ge(mid_ready, PAIRS1)
            sum_unit(STRAIGHT, U_FF + 2 * PAIRS1 - 1, PAIRS1 - 1, 3, False, True)
            statistics(LN2, True)
            spread(LN2, True)
            for half in range(2):
                for t in range(TT):
                    for c in range(4):
                        if t == 0:
                            pe.wait_ge((res_act_ready, res_pool_ready)[half], c + 1)
                        ins = nc.tensor.transpose(down[2 * t + half][:, c * P:(c + 1) * P],
                                                  res[:, 4 * half + c, t * P:(t + 1) * P], ident[:, :])
                    ins.then_inc(res_turned, 1)
            statistics(MIXPRE0, False)
            pe.wait_ge(band_landed, 16)
            pe.wait_ge(up_read, UP_INDEX[U_GLU0])
            pe.wait_ge(var_ready, MIXPRE0 + 1)
            for c in range(DC):
                gr = c // 2
                if c % 4 == 0:
                    pe.wait_ge(h_act_ready, c // 4 + 1)
                    pe.wait_ge(h_dve_ready, c // 4 + 1)
                col = (c % 2) * T
                m(diff[gr][:, col:col + BAND0], h_tok[:, 0, c * P:(c + 1) * P], band[:, gr * BAND_W:gr * BAND_W + BAND0],
                  start=(c % 2 == 0), stop=False, skip_group_check=True)
                ins = m(diff[gr][:, col + P:col + T], h_tok[:, 1, c * P:(c + 1) * P],
                        band[:, gr * BAND_W + BAND0:(gr + 1) * BAND_W], start=False, stop=True, skip_group_check=True)
                if c % 2:
                    ins.then_inc(diff_done, 1)
            n = U_POOL
            pe.wait_ge(w_lo_ready, n + 1)
            for gr in range(4):
                pe.wait_ge(x_ready, DC * X_POOL + 2 * gr + 2)
                for o in range(2):
                    for c in range(2):
                        ins = product(down[gr][:, o * T:(o + 1) * T], gr * 512 + c * 256 + o * P, n % RING,
                                      x_hi[X_POOL % 2][:, 2 * gr + c, :], x_lo[X_POOL % 2][:, 2 * gr + c, :],
                                      c == 0 and o == 0, c == 1)
                if gr < 3:
                    ins.then_inc(down_done, 1)
            ins.then_inc(unit_done, 1)
            statistics(MIXPOST0, False)
            spread(MIXPOST0, False)

            def glu(base, fill, k_pre, k_post):
                layer = (U_GLU0, U_GLU1).index(base)
                first_unit(base, fill)
                statistics(k_pre, False)
                unit(STRAIGHT, base + 1, fill)
                spread(k_pre, False)

                def units(at, j):
                    unit(at, base + 3 * j - 1, fill)
                    unit(at, base + 3 * j, fill)
                    pe.wait_ge(mid_ready, PAIRS1 + PAIRS2 * layer + at.pair(j))
                    sum_unit(at, base + 3 * j + 1, j - 1, 2, j == 1, False)

                for j in range(1, 3):
                    units(STRAIGHT, j)
                with pe.Fori(0, (PAIRS2 - 3) // 2) as i:
                    at = Looped(i, 4, 2)
                    units(at, 3)
                    units(at, 4)
                pe.wait_ge(mid_ready, PAIRS1 + PAIRS2 * (layer + 1))
                sum_unit(STRAIGHT, base + 3 * PAIRS2 - 1, PAIRS2 - 1, 2, False, True)
                statistics(k_post, False)
                spread(k_post, False)

            glu(U_GLU0, X_FFN0, FFNPRE0, FFNPOST0)
            first_unit(U_KV, X_KV)
            statistics(MIXPRE1, False)
            unit(STRAIGHT, U_KV + 1, X_KV)
            spread(MIXPRE1, False)

            def partners(n, first_tile):
                pe.wait_ge(up_read, UP_INDEX[n] + 1)
                for t in range(2):
                    ins = m(up[n % RING][:, t * T:(t + 1) * T], ccol("perm2", 0, P), proj[:, first_tile + t, :],
                            start=(t == 0), stop=True, skip_group_check=True)
                ins.then_inc(rot_done, 1)

            unit(STRAIGHT, U_Q, X_Q, DC * X_Q)
            partners(U_KV, 0)
            pe.wait_ge(up_read, UP_INDEX[U_KV + 1] + 1)
            for tl in range(2):
                for kc in range(TT):
                    ins = nc.tensor.transpose(down[2][:, tl * T + kc * P:tl * T + (kc + 1) * P],
                                              proj[:, 2 + tl, kc * P:(kc + 1) * P], ident[:, :])
            ins.then_inc(v_turned, 1)
            pe.wait_ge(rot_read, 4)
            unit(STRAIGHT, U_Q + 1, X_Q)
            partners(U_Q, 4)
            partners(U_Q + 1, 6)

            causal = [(0, 0, P), (P, 1, T)]
            causal_turn = [(0, 0), (P, P), (2 * P, 2 * P)]
            causal_attend = [(0, 0, T, 0), (1, T, P, P)]

            def score2(h):
                if h % 4 == 0:
                    pe.wait_ge(rot_ready, 3 + 2 + h // 4)
                score(16 + h, 4 + h // 2, h // 8, h % 2, causal)

            def attend2(h):
                kv = 2 * (h // 8) + h % 2
                attend(16 + h, h, X_O2, h % 2, lambda kc: v_tok2[:, kc, kv * HD:(kv + 1) * HD], causal_attend)

            def out_chunk(u, c):
                n = U_WO + u
                s = n % RING
                if c == 0:
                    pe.wait_ge(w_lo_ready, n + 1)
                    pe.wait_ge(up_read, reads_before(n))
                    pe.wait_ge(rot_read, 6 + u)
                pe.wait_ge(x_ready, DC * X_O2 + c + 1)
                for t in range(2):
                    ins = product(up[s][:, t * T:(t + 1) * T], c * UC + t * P, s, x_hi[X_O2 % 2][:, c, :],
                                  x_lo[X_O2 % 2][:, c, :], c == 0 and t == 0, c == DC - 1)
                if c == DC - 1:
                    ins.then_inc(unit_done, 1)

            out_left = [(u, c) for u in range(3) for c in range(DC)]

            def out_chunks(h, most):
                for _ in range(most):
                    ready = [(u, c) for u, c in out_left if 2 * c + 4 <= h and h >= (1, 6, 10)[u]
                             and (u, c - 1) not in out_left]
                    if ready:
                        out_left.remove(ready[0])
                        out_chunk(*ready[0])

            score2(0)
            score2(1)
            for h in range(16):
                if h + 2 < 16 and h:
                    score2(h + 2)
                if h % 2 == 0 and h < 8:
                    if h == 4:
                        pe.wait_ge(rot_read, 5)
                    tile(STRAIGHT, U_Q + 2 + h // 4, (h // 2) % 2, X_Q)
                if h == 0:
                    score2(h + 2)
                if h in (4, 8):
                    partners(U_Q + 1 + h // 4, 6 + 2 * (h // 4))
                if h == 0:
                    pe.wait_ge(v_ready, 4)
                if h >= 8 or h % 2:
                    out_chunks(h, OUT_MOST)
                turn(16 + h, causal_turn)
                if h:
                    attend2(h - 1)
            attend2(15)
            for u, c in out_left:
                out_chunk(u, c)
            unit(STRAIGHT, U_WO + 3, X_O2)
            statistics(MIXPOST1, False)
            spread(MIXPOST1, False)
            glu(U_GLU1, X_FFN1, FFNPRE1, FFNPOST1)
            for q in range(2):
                for t in range(TT):
                    b = 2 * t + q
                    for c in range(4):
                        if t == 0 and c % 2 == 0:
                            wait_added(pe, 3, 2 * q + c // 2)
                        ins = nc.tensor.transpose(down[b][:, c * P:(c + 1) * P],
                                                  res[:, 4 * q + c, t * P:(t + 1) * P], ident[:, :])
                    ins.then_inc(out_turned, 1)

        @block.vector
        def _(dve):
            v = nc.vector
            chain = Chain(dve, dve_chain)

            def split(at, n):
                s = n % RING
                dve.wait_ge(w_hi_ready, at.unit(n + 1))
                v.tensor_tensor(w_lo[s][:, :], w32[s][:, :], w_hi[s][:, :].bitcast(F32), ALU.subtract)\
                    .then_inc(w_lo_ready, 1)

            def next_split(at, n):
                if n + RING < N_UNITS:
                    split(at, n + RING)

            stats6 = scores[0][:, 0:24].rearrange("p (t s) -> p t s", t=TT)
            mv = scores[0][:, 32:36].rearrange("p (t s) -> p t s", t=TT)
            for t in range(TT):
                dve.wait_ge(x_landed[t], 16)
                for q in range(2):
                    ins = v.bn_stats(stats6[:, t, 6 * q:6 * q + 6], x_tok[:, t, q * 512:(q + 1) * 512])
            chain.link(ins)
            for t in range(TT):
                ins = v.bn_aggr(mv[:, t, :], stats6[:, t, :])
            chain.link(ins)
            v.tensor_scalar(stat[:, S_LN0, 0:2], mv[:, :, 1], LN_EPS, None, ALU.add).then_inc(ln0_var, 1)
            dve.wait_ge(ln0_rstd, 1)
            v.scalar_tensor_tensor(out=stat[:, S_LN0, 4:6], in0=mv[:, :, 0], scalar=-1.0, in1=stat[:, S_LN0, 2:4],
                                   op0=ALU.mult, op1=ALU.mult).then_inc(ln0_shift, 1)
            dve.wait_ge(ln0_shift, 1)
            v.tensor_scalar(xn_tok[:, 1, :], x_tok[:, 1, :], stat[:, S_LN0, 3:4], stat[:, S_LN0, 5:6], ALU.mult, ALU.add)\
                .then_inc(xn_ready, 1)
            split(STRAIGHT, 0)
            for c in range(DC):
                dve.wait_ge(ln0_h, c + 1)
                v.tensor_copy(x_hi[0][:, c, :], res[:, c, :]).then_inc(x_hi_ready, 1)
                dve.wait_ge(x_hi_ready, c + 1)
                v.tensor_tensor(x_lo[0][:, c, :], res[:, c, :], x_hi[0][:, c, :].bitcast(F32), ALU.subtract)\
                    .then_inc(x_ready, 1)
            split(STRAIGHT, 1)
            split(STRAIGHT, 2)

            def rotary_angles():
                dve.wait_ge(pos_landed, 16)
                dve.wait_ge(con_landed, 16)
                dve.wait_ge(par_landed, 16)
                chain.link(v.tensor_copy(angle[0], pos_i[:, :]))
                chain.link(v.tensor_scalar(angle[0], angle[0], ccol("inv_freq2"), None, ALU.mult))
                chain.link(v.tensor_scalar(angle[1], angle[0], 1.0 / (2 * np.pi), ROUND_MAGIC, ALU.mult, ALU.add))
                chain.link(v.tensor_scalar(angle[1], angle[1], ROUND_MAGIC, None, ALU.subtract))
                for part in TWO_PI_PARTS:
                    chain.link(v.scalar_tensor_tensor(out=angle[0], in0=angle[1], scalar=-part, in1=angle[0],
                                                      op0=ALU.mult, op1=ALU.add))
                v.tensor_scalar(angle[0], angle[0], PI_BELOW, -PI_BELOW, ALU.min, ALU.max).then_inc(angle_ready, 1)
                dve.wait_ge(angle_ready, 1)
                chain.link(v.tensor_scalar(angle[2], angle[0], -1.0, None, ALU.mult))
                chain.link(v.tensor_tensor(angle[2], angle[2], angle[0], ALU.max))
                v.tensor_scalar(angle[1], angle[2], -1.0, float(np.pi / 2), ALU.mult, ALU.add).then_inc(angle_ready, 1)
                v.tensor_scalar(half_gate_bias[:, :], pcol("b_in", 18, 16), 0.5, None, ALU.mult)
                v.tensor_scalar(neg_sink1[:, :], pcol("sink1", 0, HEADS_SWA), -1.0, None, ALU.mult)
                v.tensor_scalar(neg_sink2[:, :], pcol("sink2", 0, HEADS_2), -1.0, None, ALU.mult).then_inc(small_ready, 1)

            for n in range(U_QKV, U_GATE - 1):
                next_split(STRAIGHT, n)
                if n == U_QKV:
                    rotary_angles()
                if n == U_QKV + 2:
                    dve.wait_ge(trig_ready, 2)
                    chain.link(v.tensor_scalar(sin2[:, :], sin2[:, :], ccol("sign2"), None, ALU.mult))

            def values_out(r, bank, dst, tiles, col=0):
                dve.wait_ge(v_turned, r)
                src = bank[:, col:col + tiles * T].rearrange("p (a k c) -> p a k c", a=tiles, k=TT)
                v.tensor_copy(dst, src).then_inc(v_ready, 1)

            def rotate(r, bank, tiles, count, cos, sin):
                dve.wait_ge(rot_done, r)
                src = bank[:, 0:count * T].rearrange("p (t n) -> p t n", t=count)
                t_ = tmp_rot[r % 2][:, 0:count, :]
                v.tensor_tensor(t_, src, sin.unsqueeze(1).to_broadcast([P, count, T]), ALU.mult).then_inc(rot_read, 1)
                chain.link(v.tensor_tensor(proj[:, tiles:tiles + count, :], proj[:, tiles:tiles + count, :],
                                           cos.unsqueeze(1).to_broadcast([P, count, T]), ALU.mult))
                dve.wait_ge(rot_read, r)
                v.tensor_tensor(proj[:, tiles:tiles + count, :], proj[:, tiles:tiles + count, :], t_, ALU.add)\
                    .then_inc(rot_ready, 1)

            def v_dst(buf, first, tiles):
                return buf[:, :, first * P:(first + tiles) * P].rearrange("p k (a c) -> p a k c", a=tiles)

            values_out(1, down[2], v_dst(v_tok, 0, 2), 2)
            values_out(2, down[3], v_dst(v_tok, 2, 2), 2)
            for r in range(1, 4):
                if r == 3:
                    values_out(3, aux, v_dst(v_tok_swa, 0, 1), 1, col=T)
                bank, tiles, count = ((down[0], 12, 2), (down[1], 14, 2), (aux, 16, 1))[r - 1]
                rotate(r, bank, tiles, count, ccol("cos1", 0, T), ccol("sin1", 0, T))
            next_split(STRAIGHT, U_GATE - 1)

            def scores_out(h, bias, spans, neg_sink, width):
                dve.wait_ge(s_done, h + 1)
                if h >= 2:
                    dve.wait_ge(p_ready, h - 1)
                dst, src = scores[h % 2][:, 0:width], down[h % 2][:, 0:width]
                if width == 2 * T:
                    dst, src = pair_view(dst), pair_view(src)
                v.scalar_tensor_tensor(out=dst, in0=src, scalar=SCALE, in1=bias, op0=ALU.mult, op1=ALU.add)\
                    .then_inc(s_ready, 1)
                dve.wait_ge(s_ready, h + 1)
                if width == 2 * T:
                    ins = v.tensor_reduce(small[:, 0, 2 * h:2 * h + 2], dst, AX_X, ALU.max, negate=True)
                else:
                    for t, (lo, hi) in enumerate(spans):
                        ins = v.tensor_reduce(small[:, 0, 2 * h + t:2 * h + t + 1], scores[h % 2][:, lo:hi], AX_X,
                                              ALU.max, negate=True)
                if neg_sink is not None:
                    chain.link(ins)
                    ins = v.tensor_scalar(small[:, 0, 2 * h:2 * h + 2], small[:, 0, 2 * h:2 * h + 2], neg_sink, None,
                                          ALU.min)
                ins.then_inc(negmax_ready, 1)

            def denominators(h, with_sink):
                dve.wait_ge(p_ready, h + 1)
                src = small[:, 1, 2 * h:2 * h + 2]
                if with_sink:
                    chain.link(v.tensor_tensor(small[:, 3, 2 * h:2 * h + 2], src, small[:, 2, 2 * h:2 * h + 2], ALU.add))
                    src = small[:, 3, 2 * h:2 * h + 2]
                v.reciprocal(small[:, 4, 2 * h:2 * h + 2], src).then_inc(rden_ready, 1)

            def attention_out(fill, chunk):
                dve.wait_ge(x_hi_ready, hi_count[fill] + chunk + 1)
                bank = (down[3], aux)[chunk % 2]
                v.tensor_tensor(x_lo[fill % 2][:, chunk, :], bank[:, 0:T], x_hi[fill % 2][:, chunk, :].bitcast(F32),
                                ALU.subtract).then_inc(x_ready, 1)

            spans1 = [(0, T), (T, 2 * T)]

            def scores1(h):
                if h == 0:
                    dve.wait_ge(bias_ready, 1)
                    dve.wait_ge(small_ready, 1)
                if h < 8:
                    scores_out(h, shifted(region, REGION, h * BIAS_W), spans1, None, 2 * T)
                else:
                    scores_out(h, shifted(con, N_CON, CON["swa_mask"]), spans1, neg_sink1[:, h - 8:h - 7], 2 * T)

            scores1(0)
            scores1(1)
            denominators(0, False)
            for h in range(16):
                if h + 2 < 16:
                    scores1(h + 2)
                if h + 1 < 16:
                    denominators(h + 1, h + 1 >= 8)
                if h % 2 == 0 and h >= 2:
                    attention_out(X_O1, h // 2 - 1)
                    next_split(STRAIGHT, U_GATE + h // 2 - 1)
            next_split(STRAIGHT, U_GATE + 7)
            attention_out(X_O1, 7)

            for half in range(2):
                next_split(STRAIGHT, U_BRANCH + 2 * half)
                dve.wait_ge(unit_done, U_BRANCH + 2 * half + 1)
                for q in range(2):
                    gr = 2 * half + q
                    v.scalar_tensor_tensor(out=pair_view(scores[q][:, :]), in0=gates[:, 2 * gr:2 * gr + 2, :], scalar=1.0,
                                           in1=pair_view(down[q][:, :]), op0=ALU.add, op1=ALU.mult)
                dve.wait_ge(unit_done, U_BRANCH + 2 * half + 2)
                for q in range(2):
                    gr = 2 * half + q
                    chain.link(v.scalar_tensor_tensor(out=raw[:, 2 * gr:2 * gr + 2, :],
                                                      in0=gates[:, DC + 2 * gr:DC + 2 * gr + 2, :], scalar=1.0,
                                                      in1=pair_view(down[2 + q][:, :]), op0=ALU.add, op1=ALU.mult))
                    v.tensor_tensor(raw[:, 2 * gr:2 * gr + 2, :], raw[:, 2 * gr:2 * gr + 2, :], pair_view(scores[q][:, :]),
                                    ALU.add).then_inc(mixed_ready, 1)
                for q in range(2):
                    gr = 2 * half + q
                    dve.wait_ge(x_hi_ready, hi_count[X_MIXED] + gr + 1)
                    v.scalar_tensor_tensor(out=x_lo[X_MIXED % 2][:, 2 * gr:2 * gr + 2, :],
                                           in0=raw[:, 2 * gr:2 * gr + 2, :], scalar=0.5,
                                           in1=x_hi[X_MIXED % 2][:, 2 * gr:2 * gr + 2, :].bitcast(F32),
                                           op0=ALU.mult, op1=ALU.subtract).then_inc(x_ready, 2)
                next_split(STRAIGHT, U_BRANCH + 2 * half + 1)

            def rows_out(k):
                dve.wait_ge(rows_done, rows_before(k) + 1)
                v.tensor_copy(rows[k % 2][:, 0:T], aux[:, 0:T]).then_inc(rows_ready, 1)
                dve.wait_ge(rows_ready, PRE.index(k) + 1)

            def variance(k):
                dve.wait_ge(stat_done, k + 1)
                v.tensor_scalar(stat[:, k, 0:2], aux[:, 0:2], RMS_EPS, None, ALU.add).then_inc(var_ready, 1)

            def layer_norm(k, g_name, behind):
                dve.wait_ge(stat_done, k + 1)
                v.tensor_copy(stat[:, k, 6:8], aux[:, 2:4]).then_inc(mean_col, 1)
                dve.wait_ge(mean_col, k + 1)
                chain.link(v.tensor_tensor(stat[:, k, 4:6], stat[:, k, 6:8], stat[:, k, 6:8], ALU.mult))
                chain.link(v.scalar_tensor_tensor(out=stat[:, k, 0:2], in0=stat[:, k, 4:6], scalar=-1.0,
                                                  in1=aux[:, 0:2], op0=ALU.mult, op1=ALU.add))
                v.tensor_scalar(stat[:, k, 0:2], stat[:, k, 0:2], 0.0, LN_EPS, ALU.max, ALU.add).then_inc(var_ready, 1)

                def take_mean_off(gr):
                    v.tensor_tensor(raw[:, 2 * gr:2 * gr + 2, :], raw[:, 2 * gr:2 * gr + 2, :],
                                    twice(mean_bank[k][:, 0:T]), ALU.subtract).then_inc(mean_off, 1)

                dve.wait_ge(mean_done, k + 1)
                take_mean_off(0)
                dve.wait_ge(rows_done, rows_before(k) + 1)
                for c in range(DC):
                    if c % 2 == 0 and c // 2 < 3:
                        take_mean_off(c // 2 + 1)
                    dve.wait_ge(mean_off, 4 * k + c // 2 + 1)
                    v.scalar_tensor_tensor(out=raw[:, c, :], in0=raw[:, c, :], scalar=pcol(g_name, c),
                                           in1=aux[:, 0:T], op0=ALU.mult, op1=ALU.mult).then_inc(normed_ready, 1)
                    behind(c)

            def post_scale(k, g_name, index):
                dve.wait_ge(rows_done, rows_before(k) + 1)
                for c in range(DC):
                    ins = v.scalar_tensor_tensor(out=raw[:, c, :], in0=raw[:, c, :], scalar=pcol(g_name, c),
                                                 in1=aux[:, 0:T], op0=ALU.mult, op1=ALU.mult)
                    if c % 2:
                        ins.then_inc(scaled_ready, 1)
                    if c in (1, DC - 1):
                        dve.wait_ge(scaled_ready, 4 * index + c // 2 + 1)
                        v.tensor_tensor(res[:, c - 1:c + 1, :], res[:, c - 1:c + 1, :], raw[:, c - 1:c + 1, :], ALU.add)\
                            .then_inc(dve_added, 1)

            def lower(fills):
                for name, which in fills:
                    for c in range(DC):
                        dve.wait_ge(x_hi_ready, hi_count[which] + c + 1)
                        v.scalar_tensor_tensor(out=x_lo[which % 2][:, c, :], in0=res[:, c, :], scalar=pcol(name, c),
                                               in1=x_hi[which % 2][:, c, :].bitcast(F32), op0=ALU.mult,
                                               op1=ALU.subtract).then_inc(x_ready, 1)

            for gr in range(4):
                n = U_WOUT + gr
                dve.wait_ge(unit_done, n + 1)
                dve.wait_ge(res_b_ready, 4)
                v.tensor_tensor(raw[:, 2 * gr:2 * gr + 2, :], pair_view(up[n % RING][:, :]),
                                res[:, 2 * gr:2 * gr + 2, :], ALU.add).then_inc(up_read, 1)
                if gr < 3:
                    next_split(STRAIGHT, n)
                if gr >= 2:
                    add_squares(v, dve, chain, LN1, gr - 1)
            add_squares(v, dve, chain, LN1, 3)

            def lower_ln1(c):
                dve.wait_ge(x_hi_ready, hi_ready(X_LN1, c))
                v.scalar_tensor_tensor(out=x_lo[X_LN1 % 2][:, c, :], in0=raw[:, c, :], scalar=pcol("ln1_b", c),
                                       in1=x_hi[X_LN1 % 2][:, c, :].bitcast(F32), op0=ALU.add, op1=ALU.subtract)\
                    .then_inc(x_ready, 1)

            def behind_ln1(c):
                if c >= 2:
                    lower_ln1(c - 2)

            layer_norm(LN1, "ln1_g", behind_ln1)
            lower_ln1(DC - 2)
            lower_ln1(DC - 1)
            next_split(STRAIGHT, U_WOUT + 3)

            def relu_square(at, j):
                dve.wait_ge(mid_hi_ready, at.pair(j + 1))
                s = j % 3
                chain.link(v.tensor_tensor(relu_v, relu_v, relu_v, ALU.mult))
                v.tensor_tensor(mid_lo[s][:, :, :], relu_v, mid_hi[s][:, :, :].bitcast(F32), ALU.subtract)\
                    .then_inc(mid_ready, 1)

            def ff_units(at, j):
                relu_square(at, j)
                next_split(at, U_FF + 2 * j - 1)
                next_split(at, U_FF + 2 * j)

            relu_square(STRAIGHT, 0)
            next_split(STRAIGHT, U_FF)
            for j in range(1, 4):
                ff_units(STRAIGHT, j)
            with dve.Fori(0, (PAIRS1 - 4) // 3) as i:
                at = Looped(i, 3, 3)
                chain.enter(i, 3)
                for j in range(4, 7):
                    ff_units(at, j)
            chain.leave((PAIRS1 - 4) // 3)

            def sums_out(base, n_last, how, k):
                for gr in range(4):
                    if gr < 3:
                        dve.wait_ge(down_done, DOWN_BASE[base] + gr + 1)
                    else:
                        dve.wait_ge(unit_done, n_last + 1)
                    how(gr).then_inc(raw_ready, 1)
                    if gr >= 2:
                        add_squares(v, dve, chain, k, gr - 1)
                add_squares(v, dve, chain, k, 3)

            dve.wait_ge(res_b_ready, 8)
            sums_out(U_FF, U_FF + 2 * PAIRS1 - 1,
                     lambda gr: v.tensor_tensor(raw[:, 2 * gr:2 * gr + 2, :], pair_view(down[gr][:, :]),
                                                res[:, 2 * gr:2 * gr + 2, :], ALU.add), LN2)

            def behind_ln2(c):
                if c >= 6:
                    add_squares(v, dve, chain, MIXPRE0, c - 5)

            layer_norm(LN2, "ln2_g", behind_ln2)
            add_squares(v, dve, chain, MIXPRE0, 3)
            for k in range(2):
                ins = v.memset(glu_u[k][:, :, 0:2], 0.0)
            chain.link(ins)
            dve.wait_ge(stat_done, MIXPRE0 + 1)
            v.tensor_scalar(stat[:, MIXPRE0, 0:2], aux[:, 0:2], RMS_EPS, None, ALU.add).then_inc(var_ready, 1)
            dve.wait_ge(rstd_ready, MIXPRE0 + 1)
            for half in range(2):
                dve.wait_ge(res_turned, 2 * half + 2)
                v.tensor_scalar(h_tok[:, 1, half * 2 * T:(half + 1) * 2 * T], down[2 + half][:, :],
                                stat[:, MIXPRE0, 3:4], None, ALU.mult).then_inc(h_dve_ready, 1)
            for c in range(DC):
                dve.wait_ge(x_hi_ready, hi_ready(X_POOL, c | 1))
                v.scalar_tensor_tensor(out=x_lo[X_POOL % 2][:, c, :], in0=diff[c // 2][:, (c % 2) * T:(c % 2 + 1) * T],
                                       scalar=pcol("mix_pre0", c), in1=x_hi[X_POOL % 2][:, c, :].bitcast(F32),
                                       op0=ALU.mult, op1=ALU.subtract).then_inc(x_ready, 1)

            def pool_scaled(gr):
                for c in (2 * gr, 2 * gr + 1):
                    ins = v.tensor_scalar(raw[:, c, :], down[gr][:, (c % 2) * T:(c % 2 + 1) * T],
                                          pcol("pool_scale", c), None, ALU.mult)
                return ins

            sums_out(U_POOL, U_POOL, pool_scaled, MIXPOST0)
            variance(MIXPOST0)
            post_scale(MIXPOST0, "mix_post0", 0)
            lower([("ffn_pre0", X_FFN0)])
            dve.wait_ge(w_lo_ready, U_POOL + RING)
            next_split(STRAIGHT, U_POOL)

            def glu_pair(at, base, layer, j, k_pre):
                first = PAIRS2 * layer
                units = [base + (3 * j - 1 if j else 0), base + (3 * j if j else 1)]
                for kind in range(2):
                    n = units[kind]
                    dve.wait_ge(unit_done, at.unit(n + 1))
                    v.tensor_tensor(glu_u[kind][:, :, 2:T + 2], pair_view(up[n % RING][:, :]),
                                    twice(rows[k_pre % 2][:, 0:T]), ALU.mult).then_inc(up_read, 1)
                    if kind == 0 and j >= 2:
                        next_split(at, base + 3 * (j - 1) + 1)
                    if kind == 1 and 0 < j < PAIRS2 - 1:
                        next_split(at, units[0])
                    dve.wait_ge(conv_first, 2 * at.pair(first + j) + kind + 1)
                    dve.wait_ge(up_read, at.up(UP_INDEX[n] + 1))
                    for tap in (1, 0):
                        for t in range(2):
                            col = 16 * at.pair(j) + 8 * kind + 4 * t
                            ins = v.scalar_tensor_tensor(out=glu_c[kind][:, t, :], in0=glu_u[kind][:, t, tap:T + tap],
                                                         scalar=pdyn(f"conv{layer}", col + tap),
                                                         in1=glu_c[kind][:, t, :], op0=ALU.mult, op1=ALU.add)
                        if tap:
                            chain.link(ins)
                    ins.then_inc((glu_ready, conv_ready)[kind], 1)
                if j < PAIRS2 - 1:
                    next_split(at, units[1])
                dve.wait_ge(mid_hi_ready, PAIRS1 + at.pair(first + j + 1))
                v.tensor_tensor(mid_lo[j % 2][:, :, :], glu_m, mid_hi[j % 2][:, :, :].bitcast(F32), ALU.subtract)\
                    .then_inc(mid_ready, 1)

            def glu(base, layer, k_pre, k_post):
                variance(k_pre)
                next_split(STRAIGHT, base)
                rows_out(k_pre)
                for j in range(3):
                    glu_pair(STRAIGHT, base, layer, j, k_pre)
                with dve.Fori(0, GLU_ROUNDS) as i:
                    at = Looped(i, 4, 2)
                    chain.enter(i, 4)
                    glu_pair(at, base, layer, 3, k_pre)
                    glu_pair(at, base, layer, 4, k_pre)
                chain.leave(GLU_ROUNDS)
                for j in range(3 + 2 * GLU_ROUNDS, PAIRS2):
                    glu_pair(STRAIGHT, base, layer, j, k_pre)
                sums_out(base, base + 3 * PAIRS2 - 1,
                         lambda gr: v.tensor_copy(raw[:, 2 * gr:2 * gr + 2, :], pair_view(down[gr][:, :])), k_post)
                variance(k_post)

            glu(U_GLU0, 0, FFNPRE0, FFNPOST0)
            post_scale(FFNPOST0, "ffn_post0", 1)
            lower([("kv_g", X_KV)])
            dve.wait_ge(w_lo_ready, U_GLU0 + 3 * PAIRS2 + 1)
            next_split(STRAIGHT, U_GLU0 + 3 * PAIRS2 - 2)
            lower([("mix_pre1", X_Q)])
            next_split(STRAIGHT, U_GLU0 + 3 * PAIRS2 - 1)
            variance(MIXPRE1)
            next_split(STRAIGHT, U_KV)
            rows_out(MIXPRE1)

            def projected(n, tiles):
                dve.wait_ge(unit_done, n + 1)
                v.tensor_tensor(proj[:, tiles:tiles + 2, :], pair_view(up[n % RING][:, :]),
                                twice(rows[MIXPRE1 % 2][:, 0:T]), ALU.mult).then_inc(up_read, 1)
                dve.wait_ge(up_read, UP_INDEX[n] + 1)

            projected(U_KV, 0)
            projected(U_KV + 1, 2)
            next_split(STRAIGHT, U_KV + 1)
            projected(U_Q, 4)
            rotate(4, up[U_KV % RING], 0, 2, cos2[:, :], sin2[:, :])
            values_out(4, down[2], v_dst(v_tok2, 0, 2), 2)
            next_split(STRAIGHT, U_Q)
            projected(U_Q + 1, 6)
            rotate(5, up[U_Q % RING], 4, 2, cos2[:, :], sin2[:, :])
            rotate(6, up[(U_Q + 1) % RING], 6, 2, cos2[:, :], sin2[:, :])
            spans2 = [(0, P), (P, P + T)]

            def scores2(h):
                scores_out(16 + h, ccol("mask2", 0, P + T), spans2, neg_sink2[:, h:h + 1], P + T)

            scores2(0)
            scores2(1)
            denominators(16, True)
            for h in range(16):
                if h + 2 < 16:
                    scores2(h + 2)
                if h + 1 < 16:
                    denominators(16 + h + 1, True)
                if h in (4, 8):
                    rotate(6 + h // 4, up[(U_Q + 1 + h // 4) % RING], 6 + 2 * (h // 4), 2, cos2[:, :], sin2[:, :])
                if h in (2, 6):
                    projected(U_Q + 2 + h // 4, 8 + 2 * (h // 4))
                if h in (1, 3, 7):
                    next_split(STRAIGHT, U_Q + {1: 1, 3: 2, 7: 3}[h])
                if h % 2 == 0 and h >= 2:
                    attention_out(X_O2, h // 2 - 1)
            attention_out(X_O2, 7)
            for gr in range(4):
                n = U_WO + gr
                dve.wait_ge(unit_done, n + 1)
                v.tensor_copy(raw[:, 2 * gr:2 * gr + 2, :], pair_view(up[n % RING][:, :])).then_inc(up_read, 1)
                if gr < 2:
                    next_split(STRAIGHT, n)
                if gr >= 2:
                    add_squares(v, dve, chain, MIXPOST1, gr - 1)
            add_squares(v, dve, chain, MIXPOST1, 3)
            variance(MIXPOST1)
            post_scale(MIXPOST1, "mix_post1", 2)
            lower([("ffn_pre1", X_FFN1)])
            next_split(STRAIGHT, U_WO + 2)
            next_split(STRAIGHT, U_WO + 3)
            glu(U_GLU1, 1, FFNPRE1, FFNPOST1)
            post_scale(FFNPOST1, "ffn_post1", 3)
            for t in range(TT):
                dve.wait_ge(out_turned, TT + t + 1)
                v.tensor_copy(out_tok[:, t, 2 * T:4 * T], down[2 * t + 1][:, :]).then_inc(out_dve_ready, 1)


def per_partition(vec):
    return vec.reshape(-1, P).T


def head_columns(order):
    return np.concatenate([np.arange(h * HD, (h + 1) * HD) for h in order])


def weight_stream(i):
    def columns(w):
        n = w.shape[1] // UC
        return w.reshape(DC, P, n, UC).transpose(2, 1, 0, 3).reshape(n, P, UNIT)

    def row_pairs(w):
        n = w.shape[0] // (2 * P)
        return w.reshape(n, 2, P, D).transpose(0, 2, 1, 3).reshape(n, P, UNIT)

    def interleave(first, rows):
        out = list(first[0])
        for j in range(1, len(first)):
            out += [*first[j], rows[j - 1]]
        return out + [rows[len(first) - 1]]

    w_in = i["w_in"][0]
    q_b = 3 * 512
    w_in = np.concatenate([w_in[:, :q_b], w_in[:, q_b:q_b + 512][:, head_columns(SWA_ORDER)], w_in[:, q_b + 512:]], axis=1)
    units = list(columns(w_in))
    swa = i["w_branch_swa"][0][head_columns(SWA_ORDER)]
    for half in range(2):
        for w in (i["w_branch_na"][0], swa):
            units.append(w[:, half * 512:(half + 1) * 512].reshape(4, P, 512).transpose(1, 0, 2).reshape(P, UNIT))
    units += list(columns(i["w_out"][0]))
    units += interleave([[u] for u in columns(i["w_ff1"][0])], row_pairs(i["w_ff2"][0]))
    units.append(i["pool_w_2"][0].reshape(4, 2, P, 256).transpose(2, 0, 1, 3).reshape(P, UNIT))

    def glu(layer):
        w = i["ffn_w_in_2"][layer]
        return interleave(list(zip(columns(w[:, :F2]), columns(w[:, F2:]))), row_pairs(i["ffn_w_out_2"][layer]))

    units += glu(0)
    units += list(columns(i["w_kv_2"]))
    units += list(columns(i["w_q_2"][0][:, head_columns(ORDER_2)]))
    units += list(columns(i["w_o_2"][0][head_columns(ORDER_2)]))
    units += glu(1)
    return np.ascontiguousarray(np.stack(units))


def parameters(i):
    b_in = i["b_in"][0]
    q_b = 3 * 512
    b_in = np.concatenate([b_in[:q_b], b_in[q_b:q_b + 512][head_columns(SWA_ORDER)], b_in[q_b + 512:]])

    def conv(layer):
        rows = np.concatenate([i["ffn_conv_w_2"][layer], i["ffn_conv_b_2"][layer][None]])
        return rows.reshape(4, 2, PAIRS2, 2, P).transpose(4, 2, 1, 3, 0).reshape(P, 16 * PAIRS2)

    cols = {
        "ln0_g": i["ln0_g"], "ln0_b": i["ln0_b"], "b_in": b_in, "b_out": i["b_out"][0], "ln1_g": i["ln1_g"][0],
        "ln1_b": i["ln1_b"][0], "b_ff1": i["b_ff1"][0], "b_ff2": i["b_ff2"][0], "ln2_g": i["ln2_g"][0],
        "ln2_b": i["ln2_b"][0], "mix_pre0": i["mix_pre_g_2"][0], "mix_pre1": i["mix_pre_g_2"][1],
        "mix_post0": i["mix_post_g_2"][0], "mix_post1": i["mix_post_g_2"][1], "pool_scale": i["pool_scale_2"][0],
        "kv_g": i["kv_norm_g_2"], "ffn_pre0": i["ffn_pre_g_2"][0], "ffn_pre1": i["ffn_pre_g_2"][1],
        "ffn_post0": i["ffn_post_g_2"][0], "ffn_post1": i["ffn_post_g_2"][1],
    }
    blocks = {k: per_partition(v) for k, v in cols.items()}
    blocks["conv0"], blocks["conv1"] = conv(0), conv(1)
    blocks["sink1"] = np.broadcast_to(i["swa_sink"][0][SWA_ORDER], (P, HEADS_SWA))
    blocks["sink2"] = np.broadcast_to(i["sinks_2"][0][ORDER_2], (P, HEADS_2))
    return np.ascontiguousarray(np.concatenate([blocks[name] for name, _ in PARAM_WIDTHS], axis=1))


def shape_constants():
    p = np.arange(P)[:, None]
    masked = lambda ok: np.where(ok, 0.0, MASKED)
    c, ck = p % GRID_W, np.arange(GRID_W)[None]
    start = np.clip(c - KW // 2, 0, GRID_W - KW)
    j = np.arange(P + T)[None] - P
    k2 = np.concatenate([np.arange(P), np.arange(T) - P])[None]
    d = p % HD
    half = HD // 8
    inv1 = np.power(np.float32(500000.0), -(np.arange(0, 2 * half, 2, dtype=np.float32)) / np.float32(2 * half))
    ang = np.arange(T, dtype=np.float32)[None] * inv1.astype(np.float32)[d % half]
    ang = np.where(d < 2 * half, ang.astype(np.float32).reshape(P, T), np.float32(0)).astype(np.float64)
    partner1 = np.where(d < half, p + half, np.where(d < 2 * half, p - half, p))[:, 0]
    partner2 = np.where(d < HD // 2, p + HD // 2, p - HD // 2)[:, 0]
    eye = np.eye(P)
    inv2 = (1.0 / np.power(np.float32(10000.0), np.arange(0, HD, 2, dtype=np.float32) / np.float32(HD))).astype(np.float32)
    table = {
        "na_mask": masked((ck >= start) & (ck < start + KW)),
        "swa_mask": masked(np.abs(j - p) <= 128),
        "mask2": masked((p - k2 >= 0) & (p - k2 < 128)),
        "cos1": np.cos(ang), "sin1": np.sin(ang) * np.where(d < half, -1.0, 1.0),
        "perm1": eye[partner1].T, "perm2": eye[partner2].T,
        "inv_freq2": inv2[d[:, 0] % (HD // 2)][:, None], "sign2": np.where(d < HD // 2, -1.0, 1.0),
    }
    return np.ascontiguousarray(np.concatenate([table[name] for name, _ in CONST_WIDTHS], axis=1).astype(np.float32))


def pool_bands():
    tok, out = np.arange(T)[:, None], np.arange(T)[None, :]
    parts = []
    for window in POOL_WINDOWS:
        band = ((tok <= out) & (tok > out - window)) / np.minimum(out + 1, window) - (tok == out)
        parts += [band[:P, :BAND0], band[P:, P:]]
    return np.ascontiguousarray(np.concatenate(parts, axis=1).astype(np.float32))


def rpb_windows(rpb):
    out = np.zeros((HEADS_NA, 2 * GRID_ROWS - 1, 2 * GRID_W - 1), rpb.dtype)
    first = rpb.shape[1] // 2 - (GRID_ROWS - 1)
    out[:, :, GRID_W - KW:GRID_W - KW + rpb.shape[2]] = rpb[:, first:first + 2 * GRID_ROWS - 1]
    return np.stack([out[:, :, GRID_W - 1 - c:2 * GRID_W - 1 - c].reshape(HEADS_NA, -1) for c in range(GRID_W)])


def kernel(**inputs):
    import concourse.bacc as bacc
    from concourse.bass_utils import run_bass_kernel_spmd

    i = {k: np.asarray(v) for k, v in inputs.items()}
    arrays = {
        "x_in": np.ascontiguousarray(i["x"][0]),
        "w_stream": weight_stream(i),
        "params": parameters(i),
        "consts": shape_constants(),
        "bands": pool_bands(),
        "rpb": rpb_windows(i["na_rpb"][0]),
        "positions": np.ascontiguousarray(i["positions_2"][0]),
    }
    nc = bacc.Bacc("TRN2", target_bir_lowering=False, num_devices=1)
    args = [nc.dram_tensor(k, a.shape, mybir.dt.from_np(a.dtype), kind="ExternalInput").ap() for k, a in arrays.items()]
    out = nc.dram_tensor("result", (T, D), F32, kind="ExternalOutput").ap()
    build(nc, *args, out)
    r = run_bass_kernel_spmd(nc, [arrays], core_ids=[0])
    return r.results[0]["result"].reshape(1, T, D)
```
